# Optimizing a Trainium2 kernel written in Bass

```python
import jax
import jax.numpy as jnp
from jax import lax
import numpy as np
import math
import jax, jax.numpy as jnp

D_MODEL = 2048
BATCH = 1
SEQ = 256
DEPTH = 2

A_WIDTH = D_MODEL // 2
B_WIDTH = D_MODEL - A_WIDTH
A_GROUPS = 8
A_GROUP_DIM = A_WIDTH // A_GROUPS
CHUNK = 128
CONV_WIDTH = 3
ATTN_HEAD_DIM = 128
ATTN_HEADS = D_MODEL // ATTN_HEAD_DIM
DILATED_BRANCHES = ((128, 1), (512, 4), (2048, 16))
ATTN_BLOCK = 128
ROPE_THETA = 10000.0
FFN_DIM = 4 * D_MODEL
N_EVEN = (DEPTH + 1) // 2
N_ODD = DEPTH // 2
RMS_EPS = 1e-6
LN_EPS = 1e-5


def rmsnorm(x, g):
    xf = x.astype(jnp.float32)
    y = xf * lax.rsqrt(jnp.mean(xf * xf, axis=-1, keepdims=True) + RMS_EPS)
    return (y * g.astype(jnp.float32)).astype(x.dtype)

def rope(t, positions):
    dh = t.shape[-1]
    half = dh // 2
    inv_freq = ROPE_THETA ** (-jnp.arange(half, dtype=jnp.float32) * 2.0 / dh)
    ang = positions.astype(jnp.float32)[:, None] * inv_freq[None, :]
    cos = jnp.cos(ang)[None, :, None, :]
    sin = jnp.sin(ang)[None, :, None, :]
    t1 = t[..., :half].astype(jnp.float32)
    t2 = t[..., half:].astype(jnp.float32)
    out = jnp.concatenate([t1 * cos - t2 * sin, t2 * cos + t1 * sin], axis=-1)
    return out.astype(t.dtype)

def gmlp_shortconv_mixer(h, w_in, w_s, b_s, conv_w, w_out):
    bsz, s, _ = h.shape
    proj = h @ w_in
    a_u, a_v, g_b, g_c, b_x = jnp.split(
        proj, [A_WIDTH, 2 * A_WIDTH, 2 * A_WIDTH + B_WIDTH, 2 * A_WIDTH + 2 * B_WIDTH], axis=-1)

    a_u = jax.nn.gelu(a_u)
    a_v = jax.nn.gelu(a_v)
    vf = a_v.astype(jnp.float32)
    mu = jnp.mean(vf, axis=-1, keepdims=True)
    var = jnp.mean(jnp.square(vf - mu), axis=-1, keepdims=True)
    vn = ((vf - mu) * lax.rsqrt(var + LN_EPS)).astype(h.dtype)
    n_chunks = s // CHUNK
    vn = vn.reshape(bsz, n_chunks, CHUNK, A_GROUPS, A_GROUP_DIM)
    causal = jnp.tril(jnp.ones((CHUNK, CHUNK), dtype=bool))
    w_causal = jnp.where(causal[None], w_s, 0)
    mixed = jnp.einsum('gts,bnsgc->bntgc', w_causal, vn) + b_s.T[None, None, :, :, None]
    a_out = a_u * mixed.reshape(bsz, s, A_WIDTH)

    z = g_c * b_x
    zp = jnp.pad(z, ((0, 0), (CONV_WIDTH - 1, 0), (0, 0)))
    y = conv_w[0] * zp[:, 0:s]
    for tap in range(1, CONV_WIDTH):
        y = y + conv_w[tap] * zp[:, tap:tap + s]
    b_out = g_b * y

    return jnp.concatenate([a_out, b_out], axis=-1) @ w_out

def dilated_branch(q, k, v, window, dilation):
    bsz, s, nh, dh = q.shape
    n_steps = window // dilation
    blk = ATTN_BLOCK
    L = s // dilation
    nb = -(-L // blk)
    Lp = nb * blk

    def to_blocks(t):
        t = t.reshape(bsz, L, dilation, nh, dh).transpose(0, 2, 3, 1, 4)
        t = jnp.pad(t, ((0, 0), (0, 0), (0, 0), (0, Lp - L), (0, 0)))
        return t.reshape(bsz, dilation, nh, nb, blk, dh)

    def with_prev_block(t):
        prev = jnp.pad(t, ((0, 0), (0, 0), (0, 0), (1, 0), (0, 0), (0, 0)))[:, :, :, :-1]
        return jnp.concatenate([prev, t], axis=4)

    qb = to_blocks(q)
    kk = with_prev_block(to_blocks(k))
    vv = with_prev_block(to_blocks(v))

    scores = jnp.einsum('brhnqc,brhnkc->brhnqk', qb, kk).astype(jnp.float32) * (dh ** -0.5)
    qi = jnp.arange(blk)[:, None]
    ki = jnp.arange(2 * blk)[None, :]
    step = qi + blk - ki
    band = (step >= 0) & (step <= n_steps)
    key_idx = jnp.arange(nb)[:, None, None] * blk - blk + ki[None]
    mask = band[None] & (key_idx >= 0)
    scores = jnp.where(mask, scores, -jnp.inf)
    m = jnp.max(scores, axis=-1, keepdims=True)
    p = jnp.exp(scores - m)
    denom = jnp.sum(p, axis=-1, keepdims=True)
    o = jnp.einsum('brhnqk,brhnkc->brhnqc', (p / denom).astype(v.dtype), vv)
    lse = (m + jnp.log(denom))[..., 0]

    o = o.reshape(bsz, dilation, nh, Lp, dh)[:, :, :, :L].transpose(0, 3, 1, 2, 4).reshape(bsz, s, nh, dh)
    lse = lse.reshape(bsz, dilation, nh, Lp)[..., :L].transpose(0, 3, 1, 2).reshape(bsz, s, nh)
    return o, lse

def dilated_attention_mixer(h, w_qkv, w_o, positions):
    bsz, s, _ = h.shape
    qkv = h @ w_qkv
    q, k, v = jnp.split(qkv, 3, axis=-1)
    q = rope(q.reshape(bsz, s, ATTN_HEADS, ATTN_HEAD_DIM), positions)
    k = rope(k.reshape(bsz, s, ATTN_HEADS, ATTN_HEAD_DIM), positions)
    v = v.reshape(bsz, s, ATTN_HEADS, ATTN_HEAD_DIM)
    outs = []
    lses = []
    for window, dilation in DILATED_BRANCHES:
        o_i, lse_i = dilated_branch(q, k, v, window, dilation)
        outs.append(o_i.astype(jnp.float32))
        lses.append(lse_i)
    alpha = jax.nn.softmax(jnp.stack(lses, axis=0), axis=0)
    o = jnp.einsum('ibsh,ibshc->bshc', alpha, jnp.stack(outs, axis=0))
    return o.astype(h.dtype).reshape(bsz, s, ATTN_HEADS * ATTN_HEAD_DIM) @ w_o

def squared_relu_mlp(h, w_up, w_down):
    return jnp.square(jax.nn.relu(h @ w_up)) @ w_down

def first_inputs(seed: int = 0) -> dict:
    key = jax.random.key(seed)
    ks = jax.random.split(key, 14)
    f32 = jnp.float32
    d = D_MODEL
    x = jax.random.normal(ks[0], (BATCH, SEQ, d), f32)
    norm_mix_pre = 1.0 + 0.05 * jax.random.normal(ks[1], (DEPTH, d), f32)
    norm_mix_post = 1.0 + 0.05 * jax.random.normal(ks[2], (DEPTH, d), f32)
    norm_mlp_pre = 1.0 + 0.05 * jax.random.normal(ks[3], (DEPTH, d), f32)
    norm_mlp_post = 1.0 + 0.05 * jax.random.normal(ks[4], (DEPTH, d), f32)
    in_cols = 2 * A_WIDTH + 3 * B_WIDTH
    w_in_ab = jax.random.normal(ks[5], (N_EVEN, d, in_cols), f32) * d ** -0.5
    w_spatial = jax.random.normal(ks[6], (N_EVEN, A_GROUPS, CHUNK, CHUNK), f32) * (0.5 * CHUNK ** -0.5)
    b_spatial = 1.0 + 0.1 * jax.random.normal(ks[7], (N_EVEN, A_GROUPS, CHUNK), f32)
    conv_w = jax.random.normal(ks[8], (N_EVEN, CONV_WIDTH, B_WIDTH), f32) * CONV_WIDTH ** -0.5
    w_out_ab = jax.random.normal(ks[9], (N_EVEN, A_WIDTH + B_WIDTH, d), f32) * (A_WIDTH + B_WIDTH) ** -0.5
    attn_width = ATTN_HEADS * ATTN_HEAD_DIM
    w_qkv = jax.random.normal(ks[10], (N_ODD, d, 3 * attn_width), f32) * d ** -0.5
    w_o = jax.random.normal(ks[11], (N_ODD, attn_width, d), f32) * attn_width ** -0.5
    w_up = jax.random.normal(ks[12], (DEPTH, d, FFN_DIM), f32) * d ** -0.5
    w_down = jax.random.normal(ks[13], (DEPTH, FFN_DIM, d), f32) * FFN_DIM ** -0.5
    return {'x': x, 'norm_mix_pre': norm_mix_pre, 'norm_mix_post': norm_mix_post,
            'norm_mlp_pre': norm_mlp_pre, 'norm_mlp_post': norm_mlp_post,
            'w_in_ab': w_in_ab, 'w_spatial': w_spatial, 'b_spatial': b_spatial,
            'conv_w': conv_w, 'w_out_ab': w_out_ab, 'w_qkv': w_qkv, 'w_o': w_o,
            'w_up': w_up, 'w_down': w_down}

def first_block(x, norm_mix_pre, norm_mix_post, norm_mlp_pre, norm_mlp_post,
              w_in_ab, w_spatial, b_spatial, conv_w, w_out_ab, w_qkv, w_o,
              w_up, w_down):
    positions = jnp.arange(x.shape[1], dtype=jnp.int32)
    h = x
    for layer in range(DEPTH):
        hn = rmsnorm(h, norm_mix_pre[layer])
        if layer % 2 == 0:
            e = layer // 2
            mix = gmlp_shortconv_mixer(hn, w_in_ab[e], w_spatial[e], b_spatial[e], conv_w[e], w_out_ab[e])
        else:
            o = layer // 2
            mix = dilated_attention_mixer(hn, w_qkv[o], w_o[o], positions)
        h = h + rmsnorm(mix, norm_mix_post[layer])
        f = squared_relu_mlp(rmsnorm(h, norm_mlp_pre[layer]), w_up[layer], w_down[layer])
        h = h + rmsnorm(f, norm_mlp_post[layer])
    return h


ROPE_DIM = 64
Q_BLOCK = 128
NORM_EPS = 1e-6
NEG_INF = -1e30

DA_HEADS = 4
DA_QK_DIM = 64
DA_V_DIM = 128
DA_WIDTH = DA_HEADS * DA_V_DIM
DA_SUBLN_EPS = 1e-5

SW_HEADS = 16
SW_KV_HEADS = 2
SW_HEAD_DIM = 64
SW_WINDOW = 128
SW_WIDTH = SW_HEADS * SW_HEAD_DIM
SW_KV_WIDTH = SW_KV_HEADS * SW_HEAD_DIM

MLA_HEADS = 4
MLA_NOPE_DIM = 128
MLA_ROPE_DIM = 64
MLA_V_DIM = 128
MLA_Q_RANK = 512
MLA_KV_RANK = 512
MLA_WIDTH = MLA_HEADS * MLA_V_DIM

D_MIX = DA_WIDTH + SW_WIDTH + MLA_WIDTH

IN_SPLITS = (
    2 * DA_HEADS * DA_QK_DIM, 2 * DA_HEADS * DA_QK_DIM, DA_WIDTH, DA_WIDTH,
    SW_WIDTH, SW_KV_WIDTH, SW_KV_WIDTH, SW_WIDTH,
    MLA_Q_RANK, MLA_KV_RANK, MLA_ROPE_DIM, MLA_WIDTH,
)
D_IN = 5952


def rms_norm(x, w, eps=NORM_EPS):
    xf = x.astype(jnp.float32)
    xf = xf * lax.rsqrt(jnp.mean(xf * xf, axis=-1, keepdims=True) + eps)
    return xf.astype(x.dtype) * w

def rope_tables(positions, dim):
    inv_freq = jnp.power(ROPE_THETA, -jnp.arange(0, dim, 2, dtype=jnp.float32) / dim)
    ang = positions.astype(jnp.float32)[..., None] * inv_freq
    return jnp.cos(ang), jnp.sin(ang)

def apply_rope(x, cos, sin):
    half = x.shape[-1] // 2
    x1, x2 = x[..., :half], x[..., half:]
    c, s = cos.astype(x.dtype), sin.astype(x.dtype)
    return jnp.concatenate([x1 * c - x2 * s, x2 * c + x1 * s], axis=-1)

def to_query_blocks(q):
    B, S = q.shape[:2]
    nb = S // Q_BLOCK
    qb = q.reshape((B, nb, Q_BLOCK) + q.shape[2:])
    return jnp.moveaxis(qb, 1, 0), nb

def from_query_blocks(o):
    o = jnp.moveaxis(o, 0, 1)
    return o.reshape((o.shape[0], o.shape[1] * o.shape[2]) + o.shape[3:])

def diff_attention(q, k, v, lam, subln_w, lam_init):
    S = q.shape[1]
    scale = q.shape[-1] ** -0.5
    qb, nb = to_query_blocks(q)
    k_pos = jnp.arange(S)

    def block(args):
        qblk, i = args
        s = jnp.einsum('bqhcd,bkhcd->bhcqk', qblk, k).astype(jnp.float32) * scale
        q_pos = i * Q_BLOCK + jnp.arange(Q_BLOCK)
        s = jnp.where(k_pos[None, :] <= q_pos[:, None], s, NEG_INF)
        p = jax.nn.softmax(s, axis=-1)
        a = (p[:, :, 0] - lam * p[:, :, 1]).astype(v.dtype)
        return jnp.einsum('bhqk,bkhd->bqhd', a, v)

    o = from_query_blocks(lax.map(block, (qb, jnp.arange(nb))))
    o = rms_norm(o, subln_w, DA_SUBLN_EPS) * (1.0 - lam_init)
    return o.reshape(o.shape[0], o.shape[1], -1)

def causal_attention(q, k, v, scale):
    S = q.shape[1]
    qb, nb = to_query_blocks(q)
    k_pos = jnp.arange(S)

    def block(args):
        qblk, i = args
        s = jnp.einsum('bqhd,bkhd->bhqk', qblk, k).astype(jnp.float32) * scale
        q_pos = i * Q_BLOCK + jnp.arange(Q_BLOCK)
        s = jnp.where(k_pos[None, :] <= q_pos[:, None], s, NEG_INF)
        p = jax.nn.softmax(s, axis=-1).astype(v.dtype)
        return jnp.einsum('bhqk,bkhd->bqhd', p, v)

    o = from_query_blocks(lax.map(block, (qb, jnp.arange(nb))))
    return o.reshape(o.shape[0], o.shape[1], -1)

def sliding_window_attention(q, k, v, sinks):
    B, S, Hq, d = q.shape
    Hkv = k.shape[2]
    rep = Hq // Hkv
    W = SW_WINDOW
    nb = S // W
    qb = q.reshape(B, nb, W, Hkv, rep, d)

    def band(t):
        tb = t.reshape(B, nb, W, Hkv, d)
        prev = jnp.concatenate([jnp.zeros_like(tb[:, :1]), tb[:, :-1]], axis=1)
        return jnp.concatenate([prev, tb], axis=2)

    kb, vb = band(k), band(v)
    s = jnp.einsum('bnqgrd,bnkgd->bngrqk', qb, kb).astype(jnp.float32) * (d ** -0.5)
    qi = jnp.arange(W)[:, None]
    kj = jnp.arange(2 * W)[None, :]
    rel = qi + W - kj
    in_band = (rel >= 0) & (rel < W)
    has_prev = (jnp.arange(nb) > 0)[:, None, None] | (kj >= W)[None]
    mask = in_band[None] & has_prev
    s = jnp.where(mask[None, :, None, None], s, NEG_INF)
    sink = jnp.broadcast_to(sinks.astype(jnp.float32).reshape(1, 1, Hkv, rep, 1, 1),
                            s.shape[:-1] + (1,))
    p = jax.nn.softmax(jnp.concatenate([s, sink], axis=-1), axis=-1)[..., :-1].astype(v.dtype)
    o = jnp.einsum('bngrqk,bnkgd->bnqgrd', p, vb)
    return o.reshape(B, S, Hq * d)

def hybrid_layer(x, cos, sin, layer, pre_w, post_w, w_in, lq1, lk1, lq2, lk2, subln_w,
                 sinks, q_norm_w, kv_norm_w, w_uq, w_ukv, w_out):
    B, S, _ = x.shape
    h = rms_norm(x, pre_w)
    proj = h @ w_in
    offsets = np.cumsum(IN_SPLITS)[:-1].tolist()
    a_q, a_k, a_v, a_g, b_q, b_k, b_v, b_g, c_q, c_kv, c_kr, c_g = jnp.split(proj, offsets, axis=-1)

    cos4, sin4 = cos[:, :, None, :], sin[:, :, None, :]
    cos5, sin5 = cos4[:, :, :, None], sin4[:, :, :, None]

    qa = apply_rope(a_q.reshape(B, S, DA_HEADS, 2, DA_QK_DIM), cos5, sin5)
    ka = apply_rope(a_k.reshape(B, S, DA_HEADS, 2, DA_QK_DIM), cos5, sin5)
    va = a_v.reshape(B, S, DA_HEADS, DA_V_DIM)
    lam_init = 0.8 - 0.6 * math.exp(-0.3 * layer)
    lam = (jnp.exp(jnp.sum(lq1.astype(jnp.float32) * lk1.astype(jnp.float32)))
           - jnp.exp(jnp.sum(lq2.astype(jnp.float32) * lk2.astype(jnp.float32))) + lam_init)
    y_a = diff_attention(qa, ka, va, lam, subln_w, lam_init)

    qb = apply_rope(b_q.reshape(B, S, SW_HEADS, SW_HEAD_DIM), cos4, sin4)
    kb = apply_rope(b_k.reshape(B, S, SW_KV_HEADS, SW_HEAD_DIM), cos4, sin4)
    vb = b_v.reshape(B, S, SW_KV_HEADS, SW_HEAD_DIM)
    y_b = sliding_window_attention(qb, kb, vb, sinks)

    qc = (rms_norm(c_q, q_norm_w) @ w_uq).reshape(B, S, MLA_HEADS, MLA_NOPE_DIM + MLA_ROPE_DIM)
    q_nope, q_rope = qc[..., :MLA_NOPE_DIM], apply_rope(qc[..., MLA_NOPE_DIM:], cos4, sin4)
    kvc = (rms_norm(c_kv, kv_norm_w) @ w_ukv).reshape(B, S, MLA_HEADS, MLA_NOPE_DIM + MLA_V_DIM)
    k_nope, vc = kvc[..., :MLA_NOPE_DIM], kvc[..., MLA_NOPE_DIM:]
    k_rope = apply_rope(c_kr[:, :, None, :], cos4, sin4)
    qc = jnp.concatenate([q_nope, q_rope], axis=-1)
    kc = jnp.concatenate([k_nope, jnp.broadcast_to(k_rope, (B, S, MLA_HEADS, MLA_ROPE_DIM))], axis=-1)
    y_c = causal_attention(qc, kc, vc, (MLA_NOPE_DIM + MLA_ROPE_DIM) ** -0.5)

    y = jnp.concatenate([y_a, y_b, y_c], axis=-1) * jax.nn.silu(jnp.concatenate([a_g, b_g, c_g], axis=-1))
    out = y @ w_out
    return x + rms_norm(out, post_w)

def second_inputs(seed: int = 0) -> dict:
    key = jax.random.key(seed)
    ks = jax.random.split(key, 16)
    f32 = jnp.float32
    L = DEPTH

    def nrm(k, shape, scale):
        return jax.random.normal(k, shape, f32) * scale

    return {
        "x": nrm(ks[0], (BATCH, SEQ, D_MODEL), 1.0),
        "positions": jnp.broadcast_to(jnp.arange(SEQ, dtype=jnp.int32), (BATCH, SEQ)),
        "pre_norm_w": 1.0 + nrm(ks[1], (L, D_MODEL), 0.02),
        "post_norm_w": 1.0 + nrm(ks[2], (L, D_MODEL), 0.02),
        "w_in": nrm(ks[3], (L, D_MODEL, D_IN), D_MODEL ** -0.5),
        "diff_lambda_q1": nrm(ks[4], (L, DA_QK_DIM), 0.1),
        "diff_lambda_k1": nrm(ks[5], (L, DA_QK_DIM), 0.1),
        "diff_lambda_q2": nrm(ks[6], (L, DA_QK_DIM), 0.1),
        "diff_lambda_k2": nrm(ks[7], (L, DA_QK_DIM), 0.1),
        "diff_subln_w": 1.0 + nrm(ks[8], (L, DA_V_DIM), 0.02),
        "sink_logits": nrm(ks[9], (L, SW_HEADS), 0.5),
        "mla_q_norm_w": 1.0 + nrm(ks[10], (L, MLA_Q_RANK), 0.02),
        "mla_kv_norm_w": 1.0 + nrm(ks[11], (L, MLA_KV_RANK), 0.02),
        "w_uq": nrm(ks[12], (L, MLA_Q_RANK, MLA_HEADS * (MLA_NOPE_DIM + MLA_ROPE_DIM)), MLA_Q_RANK ** -0.5),
        "w_ukv": nrm(ks[13], (L, MLA_KV_RANK, MLA_HEADS * (MLA_NOPE_DIM + MLA_V_DIM)), MLA_KV_RANK ** -0.5),
        "w_out": nrm(ks[14], (L, D_MIX, D_MODEL), D_MIX ** -0.5),
    }

def second_block(x, positions, pre_norm_w, post_norm_w, w_in, diff_lambda_q1, diff_lambda_k1,
              diff_lambda_q2, diff_lambda_k2, diff_subln_w, sink_logits, mla_q_norm_w,
              mla_kv_norm_w, w_uq, w_ukv, w_out):
    cos, sin = rope_tables(positions, ROPE_DIM)
    for layer in range(DEPTH):
        x = hybrid_layer(x, cos, sin, layer, pre_norm_w[layer], post_norm_w[layer], w_in[layer],
                         diff_lambda_q1[layer], diff_lambda_k1[layer], diff_lambda_q2[layer],
                         diff_lambda_k2[layer], diff_subln_w[layer], sink_logits[layer],
                         mla_q_norm_w[layer], mla_kv_norm_w[layer], w_uq[layer], w_ukv[layer],
                         w_out[layer])
    return x


def setup_inputs(seed=0):
    out = dict(first_inputs(seed))
    for name, value in second_inputs(seed + 1).items():
        if name != "x":
            out[name + "_2"] = value
    return out


def reference(
    x, norm_mix_pre, norm_mix_post, norm_mlp_pre, norm_mlp_post, w_in_ab, w_spatial, b_spatial,
    conv_w, w_out_ab, w_qkv, w_o, w_up, w_down, positions_2, pre_norm_w_2, post_norm_w_2,
    w_in_2, diff_lambda_q1_2, diff_lambda_k1_2, diff_lambda_q2_2, diff_lambda_k2_2,
    diff_subln_w_2, sink_logits_2, mla_q_norm_w_2, mla_kv_norm_w_2, w_uq_2, w_ukv_2, w_out_2,
):
    x = first_block(
        x, norm_mix_pre, norm_mix_post, norm_mlp_pre, norm_mlp_post, w_in_ab, w_spatial,
        b_spatial, conv_w, w_out_ab, w_qkv, w_o, w_up, w_down,
    )
    return second_block(
        x, positions_2, pre_norm_w_2, post_norm_w_2, w_in_2, diff_lambda_q1_2, diff_lambda_k1_2,
        diff_lambda_q2_2, diff_lambda_k2_2, diff_subln_w_2, sink_logits_2, mla_q_norm_w_2,
        mla_kv_norm_w_2, w_uq_2, w_ukv_2, w_out_2,
    )


_drawn_inputs = setup_inputs


def setup_inputs(seed=0):
    import zlib

    import numpy as np

    out = dict(_drawn_inputs(seed))
    spreads = {}
    factors = {'pre_norm_w_2': 3.189,
     'post_norm_w_2': 4.845,
     'diff_lambda_q1_2': 3.382,
     'diff_lambda_k1_2': 3.653,
     'diff_lambda_q2_2': 8.0,
     'diff_lambda_k2_2': 4.761,
     'diff_subln_w_2': 8.0,
     'sink_logits_2': 7.836,
     'mla_q_norm_w_2': 8.0,
     'mla_kv_norm_w_2': 8.0}
    for name, (base, spread) in spreads.items():
        noise = np.random.default_rng([zlib.crc32(name.encode()), seed]).standard_normal(out[name].shape)
        drawn = base * np.exp(spread * noise) if base else spread * noise
        out[name] = jnp.asarray(drawn.astype(out[name].dtype))
    for name, factor in factors.items():
        out[name] = (out[name] * factor).astype(out[name].dtype)
    return out
```

```python
import math

import numpy as np

import concourse.bass as bass
from concourse import mybir
from contextlib import ExitStack

F32 = mybir.dt.float32
F32R = mybir.dt.float32r
I32 = mybir.dt.int32
ACT = mybir.ActivationFunctionType
ALU = mybir.AluOpType
AXIS_X = mybir.AxisListType.X

P = 128
TOKENS = 256
TB = TOKENS // P
D = 2048
KB = D // P
UNITS = 16
LAYERS = 2

A_BLOCKS = 8
HEADS = 16
FFN_QUARTERS = 4
DA_HEADS, SW_BLOCKS, MLA_HEADS = 4, 8, 4
N_MIX0 = 5 * A_BLOCKS
N_OUT = KB
N_MLP = FFN_QUARTERS * 2 * KB
N_QKV = 3 * HEADS
N_DA = 4 * DA_HEADS
N_KV = 4
N_SW = 2 * SW_BLOCKS
N_LATENT = 8
N_MLA = 2 * MLA_HEADS
N_LAYER2 = N_DA + N_KV + N_SW + N_LATENT + N_MLA + N_OUT
C_MIX0 = 0
C_OUT0 = C_MIX0 + N_MIX0
C_MLP0 = C_OUT0 + N_OUT
C_QKV = C_MLP0 + N_MLP
C_OUT1 = C_QKV + N_QKV
C_MLP1 = C_OUT1 + N_OUT
C_LAYER2 = C_MLP1 + N_MLP
CHUNKS = C_LAYER2 + LAYERS * N_LAYER2
AHEAD = 3
LOADED = CHUNKS + AHEAD

NORM_EPS = 1e-6
LN_EPS = 1e-5
SUBLN_EPS = 1e-5
MASKED = -1e30
STAT_AT, SPREAD_AT = 2, 10
LATE = 4
LATENT = 4
COLS = 3 * P

NORMS = 6
G_PRE = 0
G_POST = G_PRE + NORMS * KB
CONV = G_POST + NORMS * KB
Q_NORM = CONV + 3 * A_BLOCKS
KV_NORM = Q_NORM + LAYERS * LATENT
SUBLN = KV_NORM + LAYERS * LATENT
SINK = SUBLN + LAYERS
INV_FREQ = SINK + LAYERS * 16
SIGN = INV_FREQ + 1
LAM_INIT = SIGN + 1
N_COLS = LAM_INIT + 2 * LAYERS


def squares_pre(n):
    return 2 * KB * n


def squares_post(n):
    return 2 * KB * n + KB


def build(nc, stream, x_t, columns, lambdas, w_spatial, b_spatial, positions, tables, out):
    ctx = ExitStack()
    with ctx:
        def sb(name, shape, dt=F32):
            return ctx.enter_context(nc.sbuf_tensor(name, shape, dt))

        sems = {}

        def sem(name):
            if name not in sems:
                sems[name] = ctx.enter_context(nc.semaphore(name))
            return sems[name]

        with nc.sbuf_tensor("raw", [P, 4, UNITS * P], F32) as raw:
            pass
        w_low = sb("w_low", [P, 4, UNITS * P], F32R)
        w_high = sb("w_high", [P, 4, UNITS * P], F32R)
        xs = sb("xs", [P, KB, 2, TOKENS], F32R)
        inner = sb("inner", [P, KB, 2, TOKENS], F32R)
        h = sb("h", [P, KB, TOKENS])
        with nc.sbuf_tensor("branch", [P, KB, TOKENS], F32) as branch:
            pass
        with nc.sbuf_tensor("latent", [P, 2 * LATENT, 2, TOKENS], F32R) as latent:
            pass
        sb("branch_or_latent", [P, KB, TOKENS])
        a_v = branch[:, 0:8, :].rearrange("p a b -> p (a b)").rearrange("p (n f) -> p n f", n=TB)
        spatial = branch[:, 8:12, :].rearrange("p a b -> p (a b)").rearrange("p (g t) -> p g t", g=A_BLOCKS)
        bias_s = branch[:, 12:16, :].rearrange("p a b -> p (a b)").rearrange("p (g t) -> p g t", g=A_BLOCKS)

        col = sb("col", [P, N_COLS])
        consts = sb("consts", [P, 2 * P + 3 * COLS + 2 * TOKENS])
        ident = consts[:, 0:P]
        ones = consts[:, P:2 * P]
        mask_dil = consts[:, 2 * P:2 * P + COLS]
        mask_causal = consts[:, 2 * P + COLS:2 * P + 2 * COLS]
        mask_window = consts[:, 2 * P + 2 * COLS:2 * P + 3 * COLS]
        rope1 = consts[:, 2 * P + 3 * COLS:].rearrange("p (a t) -> p a t", a=2)
        rope_q = rope1
        rope2 = sb("rope2", [P, 2, TOKENS])
        rope_s = sb("rope_s", [P, 2, TOKENS])
        corr = sb("corr", [P, 2, TOKENS])
        y = sb("y", [P, 2, TOKENS])
        scaled = sb("scaled", [P, 2, TOKENS])
        source = sb("source", [P, 2, TOKENS])
        sq = sb("sq", [P, 2, TOKENS])
        sum_sq = sb("sum_sq", [P, TOKENS])
        step = sb("step", [P, 2, TOKENS])
        latent_sq = step
        head_sq = step[:, 0, :]
        scale_pre = sb("scale_pre", [P, TOKENS])
        scale_lat = sb("scale_lat", [P, 2, TOKENS])
        swapped = sb("swapped", [P, TOKENS])
        turned = sb("turned", [P, TOKENS])
        q_t = sb("q_t", [P, TOKENS])
        k_t = sb("k_t", [P, TOKENS])
        v_t = sb("v_t", [P, TOKENS])
        v_nat = sb("v_nat", [P, TB, P])
        kw_t = sb("kw_t", [P, TOKENS])
        vw_nat = sb("vw_nat", [P, TB, P])
        kr_t = sb("kr_t", [P, TOKENS])
        qr_t = kw_t
        gate = sb("gate", [P, TOKENS])
        tanh_g = sb("tanh_g", [P, TOKENS])
        normed = source[:, 1, :]
        diag = sb("diag", [P, TOKENS])
        prob = sb("prob", [P, 2, COLS])
        prob_t = sb("prob_t", [P, 2, COLS])
        conv_in = prob[:, 0, 0:TOKENS + 2]
        bn = prob[:, 1, 0:TB * 12].rearrange("p (n k f) -> p n k f", n=TB, k=2)
        lam_vectors = prob_t[:, :, 0:256]
        small = sb("small", [P, 72])
        minus_half = sb("minus_half", [P, TB])

        def neg_max(bank, t=None):
            return small[:, 2 * bank:2 * bank + 2] if t is None else small[:, 2 * bank + t:2 * bank + t + 1]

        def denom(bank, t=None):
            return small[:, 4 + 2 * bank:6 + 2 * bank] if t is None else small[:, 4 + 2 * bank + t:5 + 2 * bank + t]

        def inverse(bank, t=None):
            return small[:, 8 + 2 * bank:10 + 2 * bank] if t is None else small[:, 8 + 2 * bank + t:9 + 2 * bank + t]

        def exp_sink(bank):
            return small[:, 12 + 2 * bank:14 + 2 * bank]

        mean_of, root_of = small[:, 16:18], small[:, 18:20]
        av_moments, av_var, av_root = small[:, 20:24], small[:, 24:26], small[:, 26:28]
        lam_dot, lam_exp, lam = small[:, 28:32], small[:, 32:36], small[:, 36:38]
        subln_gain, neg_sinks = small[:, 38:40], small[:, 40:72]

        def psum_bank(name):
            return ctx.enter_context(nc.psum_tensor(name, [P, 512], F32))

        acc = [psum_bank(f"acc{i}") for i in range(4)]
        score = [psum_bank(f"score{i}") for i in range(2)]
        head_out = psum_bank("head_out")
        extra = psum_bank("extra")

        landed = [sem(f"landed_{s}") for s in range(4)]
        high_ready, low_ready = sem("high_ready"), sem("low_ready")
        product_done, corr_ready, summed = sem("product_done"), sem("corr_ready"), sem("summed")

        def dyn(t, i):
            return t[:, i] if isinstance(i, int) else t[:, bass.ds(i, 1)].rearrange("p a b -> p (a b)")

        def dyn2(t, i, part):
            if isinstance(i, int):
                return t[:, i, part]
            return t[:, bass.ds(i, 1), part].rearrange("p a b -> p (a b)")

        def dyn_col(t, i):
            return t[:, i:i + 1] if isinstance(i, int) else t[:, bass.ds(i, 1)]

        def column(i):
            return dyn_col(col, i)

        def latent_gain(l, i):
            return column((Q_NORM if i < LATENT else KV_NORM - LATENT) + i + LATENT * l)

        def at(value):
            return max(value, 0) if isinstance(value, int) else value

        block = ctx.enter_context(nc.Block())

        @block.sync
        def _(sp):
            def load(c, s):
                sp.dma_start(raw[:, s, :], stream[c] if isinstance(c, int)
                             else stream[bass.ds(c, 1)].rearrange("a p n -> (a p) n")).then_inc(landed[s], 16)

            sp.dma_start(col[:, :], columns).then_inc(sem("columns_landed"), 16)
            for s in range(4):
                b = s * KB // 4
                sp.dma_start(h[:, b:b + KB // 4, :], x_t[:, b:b + KB // 4, :]).then_inc(sem(f"x_landed_{s}"), 16)
                load(s, s)
            sp.dma_start(consts[:, :], tables).then_inc(sem("tables_landed"), 16)
            sp.dma_start(spatial, w_spatial).then_inc(sem("spatial_landed"), 16)
            sp.dma_start(bias_s, b_spatial).then_inc(sem("bias_landed"), 16)
            sp.dma_start(gate[:, :].bitcast(I32), positions).then_inc(sem("positions_landed"), 16)
            sp.dma_start(lam_vectors, lambdas).then_inc(sem("lambdas_landed"), 16)
            with sp.Fori(1, LOADED // 4) as i:
                for s in range(4):
                    sp.wait_ge(product_done, 4 * i + (s - 3))
                    load(4 * i + s, s)
            for c in range(LOADED - LOADED % 4, LOADED):
                sp.wait_ge(product_done, c - 3)
                load(c, c % 4)
            sp.wait_ge(sem("h_ready"), KB * 6)
            sp.dma_start(out, h[:, :, :]).then_inc(sem("out_written"), 16)
            sp.wait_ge(sem("out_written"), 16)

        @block.tensor
        def _(pe):
            def high_unit(c, s, kt, x, stop=False):
                nc.tensor.matmul(acc[s][:, :], w_high[:, s, kt * P:(kt + 1) * P], x[:, kt, :, :],
                                 start=(kt == first_of[0]), stop=False, skip_group_check=True)

            first_of = [0]

            def low_unit(s, kt, x, stop):
                return nc.tensor.matmul(acc[s][:, TOKENS:], w_low[:, s, kt * P:(kt + 1) * P], x[:, kt, 0, :],
                                        start=False, stop=stop, skip_group_check=True)

            def product(c, s, x, units=UNITS, order=None, ready=None, hooks=None, free=None):
                order = order or list(range(units))
                pe.wait_ge(high_ready, c + 1)
                pe.wait_ge(summed, at(c - 3 if free is None else free))
                first_of[0] = order[0]
                for i, kt in enumerate(order):
                    if hooks and i in hooks:
                        hooks[i]()
                    if ready:
                        ready(i)
                    high_unit(c, s, kt, x)
                pe.wait_ge(low_ready, c + 1)
                for kt in range(units):
                    mm = low_unit(s, kt, x, kt == units - 1)
                mm.then_inc(product_done, 1)

            def product_first(c, n):
                pe.wait_ge(high_ready, c + 3)
                pe.wait_ge(low_ready, c + 3)
                pe.wait_ge(summed, at(c))
                first_of[0] = 0
                for kt in range(KB):
                    pe.wait_ge(sem("xs_ready"), KB * n + kt + 1)
                    for s in range(3):
                        high_unit(c + s, s, kt, xs)
                        mm = low_unit(s, kt, xs, kt == KB - 1)
                        if kt == KB - 1:
                            mm.then_inc(product_done, 1)

            def product_early(c, ready):
                early = KB - LATE
                for s in range(3):
                    pe.wait_ge(high_ready, c + s + 1)
                    pe.wait_ge(summed, c + s - 3)
                    first_of[0] = 0
                    for kt in range(early):
                        if s == 0:
                            ready(kt)
                        high_unit(c + s, s, kt, inner)
                for s in range(3):
                    for kt in range(early, KB):
                        if s == 0:
                            ready(kt)
                        high_unit(c + s, s, kt, inner)
                    pe.wait_ge(low_ready, c + s + 1)
                    for kt in range(KB):
                        mm = low_unit(s, kt, inner, kt == KB - 1)
                    mm.then_inc(product_done, 1)

            def sum_over_features(parts, done):
                for i, part in enumerate(parts):
                    for n in range(TB):
                        mm = nc.tensor.matmul(extra[:, TOKENS + n:TOKENS + n + 1], part[:, n * P:(n + 1) * P],
                                              ones[:, 0:1], start=(i == 0 and n == 0), stop=(i == len(parts) - 1),
                                              skip_group_check=True)
                mm.then_inc(sem(done), 1)

            def spread(r):
                pe.wait_ge(sem("diag_ready"), r + 1)
                nc.tensor.matmul(extra[:, 0:TOKENS], ones, diag[:, :], start=True, stop=True)\
                    .then_inc(sem("spread_done"), 1)

            def stat_pre(n, copied):
                pe.wait_ge(sem("scale_ready"), at(copied))
                pe.wait_ge(sem("square_added"), squares_pre(n) + KB)
                sum_over_features([sum_sq[:, :]], "stat_done")

            def stat_post(m, r):
                pe.wait_ge(sem("square_added"), squares_post(m) + KB - 1)
                pe.wait_ge(sem("squared"), squares_post(m) + KB)
                sum_over_features([sum_sq[:, :], sq[:, 1, :]], "square_added")
                spread(r)

            def scores(u, bank, pairs, q_ready):
                q_ready()
                pe.wait_ge(sem("prob_t_ready"), at(u - 1))
                for (lo, hi, t0) in ((0, P, 0), (P, COLS, P)):
                    for i, (q, k) in enumerate(pairs):
                        mm = nc.tensor.matmul(score[bank][:, lo:hi], q[:, t0:t0 + P], k[:, 0:hi - lo],
                                              start=(i == 0), stop=(i == len(pairs) - 1))
                mm.then_inc(sem("scores_done"), 1)

            def turn_prob(u, bank, count=1):
                pe.wait_ge(sem("prob_ready"), u + count)
                for lo, to in ((0, 0), (P, P), (2 * P, 2 * P)):
                    mm = nc.tensor.transpose(score[bank][:, to:to + P], prob[:, bank, lo:lo + P], ident)
                mm.then_inc(sem("prob_turned"), count)

            def turn_value(v, o):
                pe.wait_ge(sem("v_scaled"), v + 1)
                pe.wait_ge(sem("out_read"), at(o))
                for n in range(TB):
                    mm = nc.tensor.transpose(head_out[:, TOKENS + n * P:TOKENS + (n + 1) * P],
                                             v_t[:, n * P:(n + 1) * P], ident)
                mm.then_inc(sem("v_turned"), 1)

            def weigh(u, bank, values, o, v=None, part=(0, P), count=1, last=True):
                pe.wait_ge(sem("prob_t_ready"), u + count)
                if v is not None:
                    pe.wait_ge(sem("v_ready"), v + 1)
                pe.wait_ge(sem("out_read"), at(o))
                a, b = part
                nc.tensor.matmul(head_out[a:b, 0:TOKENS], values[:, 0, a:b], prob_t[:, bank, 0:TOKENS],
                                 start=True, stop=False, skip_group_check=True)
                mm = nc.tensor.matmul(head_out[a:b, P:TOKENS], values[:, 1, a:b], prob_t[:, bank, TOKENS:COLS],
                                      start=False, stop=True, skip_group_check=True)
                mm.then_inc(sem("head_done"), 1)

            def out_section(c0, split0, order=None, hooks=None):
                order = order or list(range(KB))
                for s in range(4):
                    first = s == 0
                    product(c0 + s, s, inner, order=order if first else None,
                            ready=(lambda i: pe.wait_ge(sem("inner_ready"), split0 + i + 1)) if first else None,
                            hooks=hooks if first else None, free=c0 if first else None)
                with pe.Fori(1, KB // 4) as i:
                    for s in range(4):
                        product(c0 + 4 * i + s, s, inner)

            def mlp_section(c0, split0, n, r):
                def quarter(q, first):
                    c = c0 + 2 * KB * q
                    if first:
                        product_first(c, n)
                        product(c + 3, 3, xs, hooks={STAT_AT: lambda: stat_pre(n, n), SPREAD_AT: lambda: spread(r)})
                    with pe.Fori(int(first), KB // 4) as i:
                        for s in range(4):
                            product(c + 4 * i + s, s, xs)
                    c = c + KB
                    product_early(c, lambda kt: pe.wait_ge(sem("inner_ready"), split0 + KB * q + kt + 1))
                    product(c + 3, 3, inner)
                    with pe.Fori(1, KB // 4) as i:
                        for s in range(4):
                            product(c + 4 * i + s, s, inner)
                quarter(0, True)
                with pe.Fori(1, FFN_QUARTERS) as q:
                    quarter(q, False)

            product_first(C_MIX0, 0)
            pe.wait_ge(sem("tables_landed"), 16)

            def turn_av(j):
                pe.wait_ge(sem("av_gelu"), j + 1)
                pe.wait_ge(sem("av_copied"), at(j))
                for n in range(TB):
                    mm = nc.tensor.transpose(head_out[:, n * P:(n + 1) * P], (q_t, k_t)[j % 2][:, n * P:(n + 1) * P],
                                             ident)
                mm.then_inc(sem("av_turned"), 1)

            product(3, 3, xs, hooks={STAT_AT: lambda: stat_pre(0, 0), SPREAD_AT: lambda: spread(0)})
            for j in range(3):
                turn_av(j)
            for j in range(4, A_BLOCKS):
                product(j, j % 4, xs)
                turn_av(j - 1)

            def gating(j, first):
                c = A_BLOCKS + 4 * j
                product(c, 0, xs)
                if first:
                    turn_av(A_BLOCKS - 1)
                    pe.wait_ge(sem("spatial_ready"), 1)
                product(c + 1, 1, xs)
                product(c + 2, 2, xs)
                pe.wait_ge(sem("av_staged"), j + 1)
                pe.wait_ge(sem("mix_read"), at(j))
                for n in range(TB):
                    mm = nc.tensor.matmul(head_out[:, n * P:(n + 1) * P], v_nat[:, n, :], dyn(spatial, j),
                                          start=True, stop=True, skip_group_check=True)
                mm.then_inc(sem("mix_done"), 1)
                product(c + 3, 3, xs)

            gating(0, True)
            with pe.Fori(1, A_BLOCKS) as j:
                gating(j, False)
            out_section(C_OUT0, 0, order=[b for j in range(A_BLOCKS) for b in (A_BLOCKS + j, j)])
            stat_post(0, 1)
            mlp_section(C_MLP0, 16, 1, 2)
            stat_post(1, 3)

            def dilated_scores(hd, bank):
                def ready():
                    pe.wait_ge(sem("rotated"), 2 * hd + 2)
                scores(hd, bank, [(q_t, k_t)], ready)

            def dilated(i, first):
                for g in range(4):
                    hd, c = 4 * i + g, C_QKV + 12 * i + 3 * g
                    s = (3 * g) % 4
                    lone = first and g == 0
                    if lone:
                        product_first(c, 2)
                        product(c + 3, 3, xs, hooks={STAT_AT: lambda: stat_pre(2, 2), SPREAD_AT: lambda: spread(4)})
                    else:
                        if not (first and g == 1):
                            product(c, s, xs)
                        turn_value(hd - 1, hd - 1)
                        turn_prob(hd - 1, (g - 1) % 2)
                        product(c + 1, (s + 1) % 4, xs)
                        weigh(hd - 1, (g - 1) % 2, v_nat, hd - 1, v=hd - 1)
                        product(c + 2, (s + 2) % 4, xs)
                    dilated_scores(hd, g % 2)

            dilated(0, True)
            with pe.Fori(1, HEADS // 4) as i:
                dilated(i, False)

            def last_dilated_turns():
                turn_value(HEADS - 1, HEADS - 1)
                turn_prob(HEADS - 1, 1)

            out_section(C_OUT1, 80, hooks={
                6: last_dilated_turns, 13: lambda: weigh(HEADS - 1, 1, v_nat, HEADS - 1, v=HEADS - 1)})
            stat_post(2, 5)
            mlp_section(C_MLP1, 96, 3, 6)
            stat_post(3, 7)

            with pe.Fori(0, LAYERS) as l:
                c0, u0, o0, v0, r0 = C_LAYER2 + N_LAYER2 * l, 16 + 28 * l, 16 + 16 * l, 16 + 9 * l, 8 + 8 * l
                rot0 = 32 + 22 * l

                def diff_scores(hd):
                    def ready():
                        pe.wait_ge(sem("rotated"), rot0 + 2 * hd + 2)
                    for j in range(2):
                        a = j * (P // 2)
                        scores(u0 + 2 * hd + j, j, [(q_t[a:a + P // 2, :], k_t[a:a + P // 2, :])], ready)

                def diff_stat(hd):
                    pe.wait_ge(sem("head_squared"), DA_HEADS * l + hd + 1)
                    pe.wait_ge(sem("scale_ready"), 5 + 7 * l + hd)
                    sum_over_features([head_sq], "stat_done")

                def diff_turns(hd):
                    turn_value(v0 + hd, o0 + hd)
                    turn_prob(u0 + 2 * hd, 0, count=2)

                def diff_weigh(hd):
                    weigh(u0 + 2 * hd, 0, v_nat, o0 + hd, v=v0 + hd, count=2)

                def differential(hd, first):
                    c = c0 + 4 * hd
                    if first:
                        product_first(c, 4 + l)
                        product(c + 3, 3, xs, hooks={STAT_AT: lambda: stat_pre(4 + l, 4 + 7 * l),
                                                     SPREAD_AT: lambda: spread(r0)})
                    else:
                        product(c, 0, xs)
                        diff_turns(hd - 1)
                        product(c + 1, 1, xs)
                        diff_weigh(hd - 1)
                        product(c + 2, 2, xs)
                    diff_scores(hd)
                    if not first:
                        diff_stat(hd - 1)
                        product(c + 3, 3, xs)
                        spread(r0 + hd)

                differential(0, True)
                with pe.Fori(1, DA_HEADS) as hd:
                    differential(hd, False)

                c, hd = c0 + N_DA, DA_HEADS - 1
                product(c, 0, xs)
                diff_turns(hd)
                product(c + 1, 1, xs)
                diff_weigh(hd)
                product(c + 2, 2, xs)
                diff_stat(hd)
                pe.wait_ge(sem("head_squared"), DA_HEADS * l + DA_HEADS)
                turn_value(v0 + DA_HEADS, o0 + hd)
                product(c + 3, 3, xs, units=1)
                spread(r0 + DA_HEADS)

                def window_turns(b):
                    for j in range(2):
                        turn_prob(u0 + 8 + 2 * b + j, j)

                def window_weigh(b):
                    for j in range(2):
                        a = j * (P // 2)
                        weigh(u0 + 8 + 2 * b + j, j, vw_nat, o0 + DA_HEADS + b, part=(a, a + P // 2))

                def window(i, first):
                    for g in range(2):
                        b, c = 2 * i + g, c0 + N_DA + N_KV + 4 * i + 2 * g
                        lone = first and g == 0
                        product(c, 2 * g, xs)
                        product(c + 1, 2 * g + 1, xs, hooks=None if lone else {14: lambda: window_turns(b - 1)})
                        if not lone:
                            window_weigh(b - 1)

                        def ready():
                            pe.wait_ge(sem("rotated"), rot0 + 11 + b)
                        for j in range(2):
                            a = j * (P // 2)
                            scores(u0 + 8 + 2 * b + j, j, [(q_t[a:a + P // 2, :], kw_t[a:a + P // 2, :])], ready)

                window(0, True)
                with pe.Fori(1, SW_BLOCKS // 2) as i:
                    window(i, False)

                def latent_stat(i):
                    pe.wait_ge(sem("latent_squared"), 2 * LATENT * l + i + 1)
                    pe.wait_ge(sem("scale_ready"), 9 + 7 * l + i // LATENT)
                    for n in range(TB):
                        mm = nc.tensor.matmul(extra[:, TOKENS + n:TOKENS + n + 1], latent_sq[:, i % 2, n * P:(n + 1) * P],
                                              ones[:, 0:1], start=(i % LATENT == 0 and n == 0),
                                              stop=(i % LATENT == LATENT - 1), skip_group_check=True)
                    mm.then_inc(sem("latent_counted"), 1)

                c = c0 + N_DA + N_KV + N_SW
                for i in range(N_LATENT):
                    product(c + i, i % 4, xs)
                    if i == 0:
                        window_turns(SW_BLOCKS - 1)
                    if i == 1:
                        window_weigh(SW_BLOCKS - 1)
                    if i == LATENT + 1:
                        spread(r0 + 5)
                    if i:
                        latent_stat(i - 1)

                def latent_products(c, s, hd):
                    s2 = (s + 2) % 4
                    where = [acc[s][:, 0:TOKENS], acc[s][:, TOKENS:], acc[s2][:, 0:TOKENS], acc[s2][:, TOKENS:]]
                    base = [0, LATENT, LATENT, 0]
                    pe.wait_ge(high_ready, c + 1)
                    pe.wait_ge(summed, at(c - 1))
                    pe.wait_ge(sem("latent_ready"), 2 * LATENT * (l + 1))
                    for m in range(4):
                        for kt in range(LATENT):
                            w = w_high[:, s, (LATENT * m + kt) * P:(LATENT * m + kt + 1) * P]
                            for part in range(2):
                                nc.tensor.matmul(where[m], w, latent[:, base[m] + kt, part, :],
                                                 start=(m % 2 == 0 and kt == 0 and part == 0), stop=False,
                                                 skip_group_check=True)
                    pe.wait_ge(low_ready, c + 1)
                    for m in range(4):
                        for kt in range(LATENT):
                            w = w_low[:, s, (LATENT * m + kt) * P:(LATENT * m + kt + 1) * P]
                            mm = nc.tensor.matmul(where[m], w, latent[:, base[m] + kt, 0, :], start=False,
                                                  stop=(kt == LATENT - 1), skip_group_check=True)
                    mm.then_inc(product_done, 1)

                def mla_turns(hd):
                    turn_value(v0 + 5 + hd, o0 + 12 + hd)
                    turn_prob(u0 + 24 + hd, hd % 2)

                def mla_weigh(hd):
                    weigh(u0 + 24 + hd, hd % 2, v_nat, o0 + 12 + hd, v=v0 + 5 + hd)

                c = c + N_LATENT
                for hd in range(MLA_HEADS):
                    s, a = (2 * hd) % 4, (hd % 2) * (P // 2)
                    latent_products(c + 2 * hd, s, hd)
                    if hd == 0:
                        latent_stat(N_LATENT - 1)
                        spread(r0 + 6)
                    else:
                        mla_turns(hd - 1)
                    product(c + 2 * hd + 1, s + 1, xs)
                    if hd:
                        mla_weigh(hd - 1)

                    def ready():
                        pe.wait_ge(sem("rotated"), rot0 + 19 + hd)
                        pe.wait_ge(sem("nope_ready"), MLA_HEADS * l + hd + 1)
                    scores(u0 + 24 + hd, hd % 2, [(q_t, k_t), (qr_t[a:a + P // 2, :], kr_t[a:a + P // 2, :])], ready)
                hd = MLA_HEADS - 1
                out_section(c + N_MLA, 160 + KB * l, hooks={
                    6: lambda: mla_turns(hd), 13: lambda: mla_weigh(hd)})
                stat_post(4 + l, r0 + 7)

        @block.scalar
        def _(act):
            def high(c, s, units=UNITS):
                act.wait_ge(landed[s], (c - s) * 4 + 16)
                nc.scalar.activation(w_high[:, s, 0:units * P], raw[:, s, 0:units * P], ACT.Copy)\
                    .then_inc(high_ready, 1)

            def ahead(c, s, units=UNITS):
                high(c + AHEAD, (s + AHEAD) % 4, units)

            def corr_out(c, s):
                act.wait_ge(product_done, c + 1)
                act.wait_ge(summed, at(c - 1))
                nc.scalar.activation(corr[:, s % 2, :], acc[s][:, TOKENS:], ACT.Copy).then_inc(corr_ready, 1)

            def square(src, k, s, ready):
                ready()
                act.wait_ge(sem("square_added"), at(k - 1))
                nc.scalar.activation(sq[:, s % 2, :], src, ACT.Square).then_inc(sem("squared"), 1)

            def norm_input(n):
                for b in range(KB):
                    act.wait_ge(sem("h_ready"), at(KB * (n - 1) + b + 1))
                    if isinstance(n, int) and n == 0 and b % 4 == 0:
                        act.wait_ge(sem(f"x_landed_{b // 4}"), 16)
                        if b // 4 < AHEAD:
                            high(b // 4, b // 4)
                    nc.scalar.activation(xs[:, b, 0, :], h[:, b, :], ACT.Copy,
                                         scale=column(G_PRE + KB * n + b)).then_inc(sem("xs_high"), 1)
                    square(h[:, b, :], squares_pre(n) + b, b, lambda: None)

            def out_section(c0, k0):
                def four(i):
                    for s in range(4):
                        c = c0 + 4 * i + s
                        corr_out(c, s)
                        if s < 3:
                            ahead(c, s)
                        square(dyn(branch, 4 * i + s), k0 + 4 * i + s, s, lambda: act.wait_ge(summed, c + 1))
                        if s == 3:
                            ahead(c, s)
                with act.Fori(0, KB // 4) as i:
                    four(i)

            def split_high(src, split, b, s):
                act.wait_ge(sem("source_ready"), src + 1)
                nc.scalar.activation(dyn2(inner, b, 0), source[:, s, :], ACT.Copy).then_inc(sem("inner_high"), 1)

            def mlp_section(c0, src0, split0, m):
                def quarter(q, last):
                    with act.Fori(0, KB // 4) as i:
                        for s in range(4):
                            j = 4 * i + s
                            c = c0 + 2 * KB * q + j
                            corr_out(c, s)
                            ahead(c, s)
                            split_high(src0 + KB * q + j, split0 + KB * q + j, j, s % 2)
                    with act.Fori(0, KB // 4) as i:
                        for s in range(4):
                            b = 4 * i + s
                            c = c0 + 2 * KB * q + KB + b
                            corr_out(c, s)
                            if s < 3 or not last:
                                ahead(c, s)
                            if last:
                                square(dyn(branch, b), squares_post(m) + b, s,
                                       lambda: act.wait_ge(sem("down_added"), 3 * KB * (m // 2) + 2 * KB + b + 1))
                                if s == 3:
                                    ahead(c, s)
                with act.Fori(0, FFN_QUARTERS - 1) as q:
                    quarter(q, False)
                quarter(FFN_QUARTERS - 1, True)

            def swap(rot, c, s, half):
                act.wait_ge(summed, c + 1)
                act.wait_ge(sem("rot_sin"), at(rot))
                exchange(y[:, s % 2, :], half)

            def exchange(src, half):
                for a in range(0, P, half):
                    b = a + half if (a // half) % 2 == 0 else a - half
                    cp = nc.scalar.activation(swapped[a:a + half, :], src[b:b + half, :], ACT.Copy)
                cp.then_inc(sem("swapped_ready"), 1)

            def exp_scores(u, bank, sink=None):
                act.wait_ge(sem("negmax_ready"), u + 1)
                for t, (lo, hi) in enumerate(((0, P), (P, COLS))):
                    nc.scalar.activation(prob[:, bank, lo:hi], prob[:, bank, lo:hi], ACT.Exp,
                                         bias=neg_max(bank, t), accum_out=denom(bank, t)).then_inc(sem("exp_ready"), 1)
                if sink is not None:
                    nc.scalar.activation(exp_sink(bank), neg_max(bank), ACT.Exp, bias=sink)\
                        .then_inc(sem("sink_ready"), 1)

            def copy_prob(u, bank, count=1):
                act.wait_ge(sem("prob_turned"), u + count)
                nc.scalar.activation(prob_t[:, bank, :], score[bank][:, 0:COLS], ACT.Copy)\
                    .then_inc(sem("prob_t_ready"), count)

            def copy_value(v, to):
                act.wait_ge(sem("v_turned"), v + 1)
                nc.scalar.activation(to[:, :, :], head_out[:, TOKENS:].rearrange("p (n f) -> p n f", n=TB), ACT.Copy)\
                    .then_inc(sem("v_ready"), 1)

            act.wait_ge(sem("columns_landed"), 16)
            norm_input(0)
            def copy_av(j):
                act.wait_ge(sem("av_turned"), j + 1)
                nc.scalar.activation(a_v[:, :, j * P:(j + 1) * P],
                                     head_out[:, 0:TOKENS].rearrange("p (n f) -> p n f", n=TB), ACT.Copy)\
                    .then_inc(sem("av_copied"), 1)

            for j in range(A_BLOCKS):
                corr_out(j, j % 4)
                ahead(j, j % 4)
                act.wait_ge(sem("av_scaled"), j + 1)
                act.wait_ge(sem("av_turned"), at(j - 1))
                nc.scalar.activation((q_t, k_t)[j % 2][:, :], scaled[:, j % 2, :], ACT.Gelu_apprx_tanh)\
                    .then_inc(sem("av_gelu"), 1)
                if j:
                    copy_av(j - 1)

            def gating(j, first):
                c = A_BLOCKS + 4 * j
                for s in range(4):
                    corr_out(c + s, s)
                    if first and s == 0:
                        copy_av(A_BLOCKS - 1)
                    if s == 3:
                        act.wait_ge(sem("au_scaled"), j + 1)
                        act.wait_ge(sem("source_ready"), at(2 * j))
                        nc.scalar.activation(k_t[:, :], scaled[:, 1, :], ACT.Gelu_apprx_tanh)\
                            .then_inc(sem("au_gelu"), 1)
                    ahead(c + s, s)
                    if s == 2:
                        split_high(2 * j, 2 * j, A_BLOCKS + j, 0)
                    if s == 3:
                        split_high(2 * j + 1, 2 * j + 1, j, 1)

            gating(0, True)
            with act.Fori(1, A_BLOCKS) as j:
                gating(j, False)
            out_section(C_OUT0, squares_post(0))
            norm_input(1)
            for i in range(2):
                act.wait_ge(sem("angle_ready"), i + 1)
                nc.scalar.activation(rope2[:, i, :], rope2[:, i, :], ACT.Sin).then_inc(sem("sine_ready"), 1)
            act.wait_ge(sem("dots_ready"), 1)
            nc.scalar.activation(lam_exp, lam_dot, ACT.Exp).then_inc(sem("lam_exp_ready"), 1)
            mlp_section(C_MLP0, 16, 16, 1)
            norm_input(2)

            def head_high(hd):
                act.wait_ge(sem("head_done"), hd + 1)
                nc.scalar.activation(dyn2(inner, hd, 0), head_out[:, 0:TOKENS], ACT.Copy)\
                    .then_inc(sem("inner_high"), 1)

            def dilated(i, first):
                for g in range(4):
                    hd, c = 4 * i + g, C_QKV + 12 * i + 3 * g
                    s = (3 * g) % 4
                    lone = first and g == 0
                    corr_out(c, s)
                    ahead(c, s)
                    swap(2 * hd, c, s, P // 2)
                    if not lone:
                        copy_value(hd - 1, v_nat)
                        copy_prob(hd - 1, (g - 1) % 2)
                    corr_out(c + 1, (s + 1) % 4)
                    ahead(c + 1, (s + 1) % 4)
                    swap(2 * hd + 1, c + 1, (s + 1) % 4, P // 2)
                    if not lone:
                        head_high(hd - 1)
                    corr_out(c + 2, (s + 2) % 4)
                    ahead(c + 2, (s + 2) % 4)
                    exp_scores(hd, g % 2)

            dilated(0, True)
            with act.Fori(1, HEADS // 4) as i:
                dilated(i, False)
            copy_value(HEADS - 1, v_nat)
            copy_prob(HEADS - 1, 1)
            head_high(HEADS - 1)
            out_section(C_OUT1, squares_post(2))
            norm_input(3)
            mlp_section(C_MLP1, 80, 96, 3)
            norm_input(4)

            with act.Fori(0, LAYERS) as l:
                c0, u0, o0, v0 = C_LAYER2 + N_LAYER2 * l, 16 + 28 * l, 16 + 16 * l, 16 + 9 * l
                rot0, gate0, src0, split0, done0 = 32 + 22 * l, 16 * l, 144 + 16 * l, 160 + 16 * l, 16 + 24 * l

                def gate_tanh(g):
                    act.wait_ge(sem("gate_scaled"), gate0 + g + 1)
                    nc.scalar.activation(tanh_g[:, :], scaled[:, 1, :], ACT.Tanh, scale=0.5)\
                        .then_inc(sem("tanh_ready"), 1)

                def diff_square(hd):
                    act.wait_ge(sem("head_done"), done0 + hd + 1)
                    nc.scalar.activation(head_sq[:, :], head_out[:, 0:TOKENS], ACT.Square)\
                        .then_inc(sem("head_squared"), 1)

                def differential(hd, first):
                    c = c0 + 4 * hd
                    corr_out(c, 0)
                    ahead(c, 0)
                    swap(rot0 + 2 * hd, c, 0, 32)
                    if not first:
                        copy_value(v0 + hd - 1, v_nat)
                        copy_prob(u0 + 2 * hd - 2, 0, count=2)
                    corr_out(c + 1, 1)
                    ahead(c + 1, 1)
                    swap(rot0 + 2 * hd + 1, c + 1, 1, 32)
                    if not first:
                        diff_square(hd - 1)
                    corr_out(c + 2, 2)
                    ahead(c + 2, 2)
                    for j in range(2):
                        exp_scores(u0 + 2 * hd + j, j)
                    corr_out(c + 3, 3)
                    ahead(c + 3, 3)
                    gate_tanh(hd)
                    if not first:
                        split_high(src0 + hd - 1, split0 + hd - 1, hd - 1, 0)

                differential(0, True)
                with act.Fori(1, DA_HEADS) as hd:
                    differential(hd, False)

                c, hd = c0 + N_DA, DA_HEADS - 1
                corr_out(c, 0)
                ahead(c, 0, units=1)
                swap(rot0 + 8, c, 0, 32)
                copy_value(v0 + hd, v_nat)
                copy_prob(u0 + 2 * hd, 0, count=2)
                corr_out(c + 1, 1)
                ahead(c + 1, 1)
                diff_square(hd)
                corr_out(c + 2, 2)
                ahead(c + 2, 2)
                swap(rot0 + 9, c + 2, 2, 32)
                copy_value(v0 + DA_HEADS, vw_nat)
                corr_out(c + 3, 3)
                ahead(c + 3, 3)
                split_high(src0 + hd, split0 + hd, hd, 0)

                def window_copies(b):
                    for j in range(2):
                        copy_prob(u0 + 8 + 2 * b + j, j)

                def window(i, first):
                    for g in range(2):
                        b, c = 2 * i + g, c0 + N_DA + N_KV + 4 * i + 2 * g
                        lone = first and g == 0
                        corr_out(c, 2 * g)
                        ahead(c, 2 * g)
                        swap(rot0 + 10 + b, c, 2 * g, 32)
                        if not lone:
                            window_copies(b - 1)
                        corr_out(c + 1, 2 * g + 1)
                        ahead(c + 1, 2 * g + 1)
                        gate_tanh(DA_HEADS + b)
                        for j in range(2):
                            exp_scores(u0 + 8 + 2 * b + j, j, sink=column(SINK + 16 * l + 8 * j + b))
                        if not lone:
                            split_high(src0 + DA_HEADS + b - 1, 0, DA_HEADS + b - 1, 0)

                window(0, True)
                with act.Fori(1, SW_BLOCKS // 2) as i:
                    window(i, False)

                c = c0 + N_DA + N_KV + N_SW
                for i in range(N_LATENT):
                    corr_out(c + i, i % 4)
                    ahead(c + i, i % 4)
                    if i == 0:
                        window_copies(SW_BLOCKS - 1)
                    act.wait_ge(sem("latent_scaled"), N_LATENT * l + i + 1)
                    nc.scalar.activation(latent[:, i, 0, :], scaled[:, i % 2, :], ACT.Copy,
                                         scale=latent_gain(l, i)).then_inc(sem("latent_high"), 1)
                    if i > 1:
                        act.wait_ge(sem("latent_counted"), N_LATENT * l + i - 1)
                    nc.scalar.activation(latent_sq[:, i % 2, :], scaled[:, i % 2, :], ACT.Square)\
                        .then_inc(sem("latent_squared"), 1)
                    if i == 1:
                        split_high(src0 + 11, 0, 11, 0)

                c = c + N_LATENT
                for hd in range(MLA_HEADS):
                    s = (2 * hd) % 4
                    corr_out(c + 2 * hd, (s + 2) % 4)
                    act.wait_ge(sem("rot_sin"), rot0 + 18 + hd)
                    exchange(acc[(s + 2) % 4][:, TOKENS:], 32)
                    if hd:
                        copy_value(v0 + 4 + hd, v_nat)
                        copy_prob(u0 + 23 + hd, (hd - 1) % 2)
                    ahead(c + 2 * hd, s)
                    corr_out(c + 2 * hd + 1, s + 1)
                    ahead(c + 2 * hd + 1, s + 1)
                    gate_tanh(12 + hd)
                    exp_scores(u0 + 24 + hd, hd % 2)
                    if hd:
                        split_high(src0 + 11 + hd, 0, 11 + hd, 0)
                copy_value(v0 + 8, v_nat)
                copy_prob(u0 + 27, 1)
                split_high(src0 + 15, 0, 15, 0)
                out_section(c + N_MLA, squares_post(4 + l))
                norm_input(5 + l)

        @block.gpsimd
        def _(pool):
            def add_squares(k0, stats=None, count=KB):
                pool.wait_ge(sem("squared"), k0 + 2)
                pool.wait_ge(sem("square_added"), k0)
                if stats is not None:
                    pool.wait_ge(sem("stat_done"), stats)
                nc.gpsimd.tensor_tensor(sum_sq[:, :], sq[:, 0, :], sq[:, 1, :], ALU.add)\
                    .then_inc(sem("square_added"), 2)
                for b in range(2, count):
                    pool.wait_ge(sem("squared"), k0 + b + 1)
                    pool.wait_ge(sem("square_added"), k0 + b)
                    nc.gpsimd.tensor_tensor(sum_sq[:, :], sum_sq[:, :], sq[:, b % 2, :], ALU.add)\
                        .then_inc(sem("square_added"), 1)

            def root(r):
                pool.wait_ge(sem("mean_ready"), r + 1)
                nc.gpsimd.tensor_tensor(root_of, mean_of, minus_half[:, :], ALU.pow).then_inc(sem("root_ready"), 1)

            nc.gpsimd.memset(minus_half[:, :], -0.5).then_inc(sem("half_set"), 1)
            nc.gpsimd.memset(conv_in[:, 0:2], 0.0).then_inc(sem("pad_set"), 1)
            pool.wait_ge(sem("half_set"), 1)
            add_squares(squares_pre(0))
            root(0)
            pool.wait_ge(sem("spatial_landed"), 16)
            nc.gpsimd.affine_select(out=spatial, in_=spatial, compare_op=ALU.is_ge, fill=0.0, base=0,
                                    pattern=[[0, A_BLOCKS], [1, P]], channel_multiplier=-1)\
                .then_inc(sem("spatial_ready"), 1)
            pool.wait_ge(sem("av_var_ready"), 1)
            nc.gpsimd.tensor_tensor(av_root, av_var, minus_half[:, :], ALU.pow).then_inc(sem("av_root_ready"), 1)
            for m in range(4):
                add_squares(squares_post(m), m + 1, KB - 1)
                root(2 * m + 1)
                add_squares(squares_pre(m + 1))
                if m < 3:
                    root(2 * m + 2)
            with pool.Fori(0, LAYERS) as l:
                for i in range(7):
                    root(8 + 8 * l + i)
                add_squares(squares_post(4 + l), 5 * (l + 1), KB - 1)
                root(8 + 8 * l + 7)
                add_squares(squares_pre(5 + l))

        @block.vector
        def _(dve):
            V = nc.vector

            def low(c, s, units=UNITS):
                dve.wait_ge(high_ready, c + 1)
                V.tensor_tensor(w_low[:, s, 0:units * P], raw[:, s, 0:units * P], w_high[:, s, 0:units * P],
                                ALU.subtract).then_inc(low_ready, 1)

            def ahead(c, s, units=UNITS):
                low(c + AHEAD, (s + AHEAD) % 4, units)

            def sum_halves(c, s, to=None):
                dve.wait_ge(corr_ready, c + 1)
                V.tensor_tensor(y[:, s % 2, :] if to is None else to, acc[s][:, 0:TOKENS], corr[:, s % 2, :], ALU.add)\
                    .then_inc(summed, 1)

            def scale_by(to, c, s, scale, done):
                dve.wait_ge(summed, c + 1)
                V.tensor_tensor(to, y[:, s % 2, :], scale, ALU.mult).then_inc(sem(done), 1)

            def mean(r, count, eps, stat_sem, value):
                dve.wait_ge(sem(stat_sem), value)
                V.tensor_scalar(mean_of, extra[:, TOKENS:TOKENS + TB], 1.0 / count, eps, ALU.mult, ALU.add)\
                    .then_inc(sem("mean_ready"), 1)
                dve.wait_ge(sem("root_ready"), r + 1)
                for n in range(TB):
                    op = V.tensor_scalar(diag[:, n * P:(n + 1) * P], ident, root_of[:, n:n + 1], None, ALU.mult)
                op.then_inc(sem("diag_ready"), 1)

            def scale_out(r, copied, to):
                dve.wait_ge(sem("spread_done"), r + 1)
                V.tensor_copy(to, extra[:, 0:TOKENS]).then_inc(sem("scale_ready"), 1)
                dve.wait_ge(sem("scale_ready"), copied + 1)

            def xs_low(n, b):
                dve.wait_ge(sem("xs_high"), KB * n + b + 1)
                V.scalar_tensor_tensor(out=xs[:, b, 1, :], in0=h[:, b, :], scalar=column(G_PRE + KB * n + b),
                                       in1=xs[:, b, 0, :], op0=ALU.mult, op1=ALU.subtract)\
                    .then_inc(sem("xs_ready"), 1)

            def norm(m, n, r, c):
                mean(r, D, NORM_EPS, "square_added", squares_post(m) + KB)
                low(c + 2, 2)
                dve.wait_ge(sem("spread_done"), r + 1)
                for b in range(KB):
                    k = KB * m + b
                    V.scalar_tensor_tensor(out=step[:, b % 2, :], in0=branch[:, b, :],
                                           scalar=column(G_POST + KB * m + b), in1=extra[:, 0:TOKENS],
                                           op0=ALU.mult, op1=ALU.mult).then_inc(sem("step_ready"), 1)
                    dve.wait_ge(sem("step_ready"), k + 1)
                    V.tensor_tensor(h[:, b, :], h[:, b, :], step[:, b % 2, :], ALU.add).then_inc(sem("h_ready"), 1)
                    if b:
                        xs_low(n, b - 1)
                xs_low(n, KB - 1)

            def norm_scale(r, sd, copied):
                mean(r, D, NORM_EPS, "stat_done", sd + 1)
                scale_out(r, copied, scale_pre[:, :])

            def split_low(split, b, s):
                dve.wait_ge(sem("inner_high"), split + 1)
                V.tensor_tensor(dyn2(inner, b, 1), source[:, s, :], dyn2(inner, b, 0), ALU.subtract)\
                    .then_inc(sem("inner_ready"), 1)

            def out_section(c0):
                def four(i, last):
                    for s in range(4):
                        c = c0 + 4 * i + s
                        sum_halves(c, s, dyn(branch, 4 * i + s))
                        if s < 3 or not last:
                            ahead(c, s)
                with dve.Fori(0, KB // 4 - 1) as i:
                    four(i, False)
                four(KB // 4 - 1, True)

            def mlp_section(c0, split0, up0):
                def quarter(q, first, last):
                    with dve.Fori(0, KB // 4) as i:
                        for s in range(4):
                            j = 4 * i + s
                            c = c0 + 2 * KB * q + j
                            up = up0 + KB * q + j
                            sum_halves(c, s)
                            scale_by(scaled[:, s % 2, :], c, s, scale_pre[:, :], "up_scaled")
                            dve.wait_ge(sem("up_scaled"), up + 1)
                            V.scalar_tensor_tensor(out=source[:, s % 2, :], in0=scaled[:, s % 2, :], scalar=0.0,
                                                   in1=scaled[:, s % 2, :], op0=ALU.max, op1=ALU.mult)\
                                .then_inc(sem("source_ready"), 1)
                            ahead(c, s)
                            split_low(split0 + KB * q + j, j, s % 2)
                    def four(i, last_four):
                        for s in range(4):
                            b = 4 * i + s
                            c = c0 + 2 * KB * q + KB + b
                            if first:
                                sum_halves(c, s, dyn(branch, b))
                            else:
                                sum_halves(c, s)
                                dve.wait_ge(summed, c + 1)
                                V.tensor_tensor(dyn(branch, b), dyn(branch, b), y[:, s % 2, :], ALU.add)\
                                    .then_inc(sem("down_added"), 1)
                            if not (last_four and s == 3):
                                ahead(c, s)
                    with dve.Fori(0, KB // 4 - int(last)) as i:
                        four(i, False)
                    if last:
                        four(KB // 4 - 1, True)
                quarter(0, True, False)
                with dve.Fori(1, FFN_QUARTERS - 1) as q:
                    quarter(q, False, False)
                quarter(FFN_QUARTERS - 1, False, True)

            def rotate_cos(c, s, table):
                dve.wait_ge(summed, c + 1)
                V.tensor_tensor(scaled[:, 0, :], y[:, s % 2, :], table[:, 0, :], ALU.mult).then_inc(sem("rot_cos"), 1)

            def rotate(rot, cos, table, to, free):
                dve.wait_ge(sem("swapped_ready"), rot + 1)
                V.tensor_tensor(turned[:, :], swapped[:, :], table[:, 1, :], ALU.mult).then_inc(sem("rot_sin"), 1)
                dve.wait_ge(sem("rot_sin"), rot + 1)
                dve.wait_ge(sem("rot_cos"), cos + 1)
                free()
                V.tensor_tensor(to[:, :], scaled[:, 0, :], turned[:, :], ALU.add).then_inc(sem("rotated"), 1)

            def mask_max(u, bank, mask, scale, neg_sink=None):
                dve.wait_ge(sem("scores_done"), u + 1)
                dve.wait_ge(sem("prob_turned"), at(u - 1))
                V.scalar_tensor_tensor(out=prob[:, bank, :], in0=score[bank][:, 0:COLS], scalar=scale, in1=mask,
                                       op0=ALU.mult, op1=ALU.add).then_inc(sem("masked"), 1)
                dve.wait_ge(sem("masked"), u + 1)
                for t, (lo, hi) in enumerate(((0, P), (P, COLS))):
                    op = V.tensor_reduce(neg_max(bank, t), prob[:, bank, lo:hi], AXIS_X, ALU.max, negate=True)
                if neg_sink is not None:
                    op.then_inc(sem("window_maxed"), 1)
                    dve.wait_ge(sem("window_maxed"), neg_sink[1] + 1)
                    op = V.tensor_scalar(neg_max(bank), neg_max(bank), neg_sink[0], None, ALU.min)
                op.then_inc(sem("negmax_ready"), 1)

            def normalise(u, bank, sink=None):
                dve.wait_ge(sem("exp_ready"), 2 * u + 2)
                if sink is not None:
                    dve.wait_ge(sem("sink_ready"), sink + 1)
                    V.tensor_tensor(denom(bank), denom(bank), exp_sink(bank), ALU.add).then_inc(sem("sink_added"), 1)
                    dve.wait_ge(sem("sink_added"), sink + 1)
                V.reciprocal(inverse(bank), denom(bank)).then_inc(sem("inverse_ready"), 1)
                dve.wait_ge(sem("inverse_ready"), u + 1)
                for t, (lo, hi) in enumerate(((0, P), (P, COLS))):
                    op = V.tensor_scalar(prob[:, bank, lo:hi], prob[:, bank, lo:hi], inverse(bank, t), None, ALU.mult)
                op.then_inc(sem("prob_ready"), 1)

            dve.wait_ge(sem("columns_landed"), 16)
            for b in range(KB):
                if b % 4 == 0 and b // 4 < AHEAD:
                    low(b // 4, b // 4)
                xs_low(0, b)
            norm_scale(0, 0, 0)

            for j in range(A_BLOCKS):
                sum_halves(j, j % 4)
                dve.wait_ge(sem("av_gelu"), at(j - 1))
                scale_by(scaled[:, j % 2, :], j, j, scale_pre[:, :], "av_scaled")
                ahead(j, j % 4)

            def gating(j, first):
                c = A_BLOCKS + 4 * j
                sum_halves(c, 0)
                scale_by(v_t[:, :], c, 0, scale_pre[:, :], "gc_ready")
                ahead(c, 0)
                if first:
                    dve.wait_ge(sem("av_copied"), A_BLOCKS)
                    for n in range(TB):
                        for k in range(2):
                            V.bn_stats(bn[:, n, k, :], a_v[:, n, k * 512:(k + 1) * 512]).then_inc(sem("av_stats"), 1)
                    dve.wait_ge(sem("av_stats"), 4)
                    for n in range(TB):
                        V.bn_aggr(av_moments[:, 2 * n:2 * n + 2], bn[:, n, :, :]).then_inc(sem("av_moments"), 1)
                    dve.wait_ge(sem("av_moments"), 2)
                    V.tensor_scalar(av_var, av_moments[:, 1:4:2], LN_EPS, None, ALU.add).then_inc(sem("av_var_ready"), 1)
                    dve.wait_ge(sem("av_root_ready"), 1)
                    dve.wait_ge(sem("bias_landed"), 16)
                    dve.wait_ge(sem("pad_set"), 1)
                sum_halves(c + 1, 1)
                scale_by(scaled[:, 1, :], c + 1, 1, scale_pre[:, :], "bx_scaled")
                dve.wait_ge(sem("bx_scaled"), j + 1)
                dve.wait_ge(sem("gc_ready"), j + 1)
                V.tensor_tensor(conv_in[:, 2:], scaled[:, 1, :], v_t[:, :], ALU.mult).then_inc(sem("conv_in_ready"), 1)
                dve.wait_ge(sem("conv_in_ready"), j + 1)
                V.tensor_scalar(q_t[:, :], conv_in[:, 0:TOKENS], column(CONV + j), None, ALU.mult)\
                    .then_inc(sem("tap"), 1)
                for tap in (1, 2):
                    dve.wait_ge(sem("tap"), 3 * j + tap)
                    V.scalar_tensor_tensor(out=q_t[:, :], in0=conv_in[:, tap:tap + TOKENS],
                                           scalar=column(CONV + A_BLOCKS * tap + j), in1=q_t[:, :],
                                           op0=ALU.mult, op1=ALU.add).then_inc(sem("tap"), 1)
                ahead(c + 1, 1)
                dve.wait_ge(sem("mix_done"), at(j))
                for n in range(TB):
                    src = a_v[:, n, :].rearrange("p (j f) -> p j f", f=P)
                    op = V.tensor_scalar(v_nat[:, n, :], dyn(src, j), av_moments[:, 2 * n:2 * n + 1],
                                         av_root[:, n:n + 1], ALU.subtract, ALU.mult)
                op.then_inc(sem("av_staged"), 1)
                sum_halves(c + 2, 2)
                scale_by(scaled[:, 0, :], c + 2, 2, scale_pre[:, :], "gb_scaled")
                dve.wait_ge(sem("gb_scaled"), j + 1)
                dve.wait_ge(sem("tap"), 3 * j + 3)
                V.tensor_tensor(source[:, 0, :], scaled[:, 0, :], q_t[:, :], ALU.mult).then_inc(sem("source_ready"), 1)
                ahead(c + 2, 2)
                split_low(2 * j, A_BLOCKS + j, 0)
                sum_halves(c + 3, 3)
                scale_by(scaled[:, 1, :], c + 3, 3, scale_pre[:, :], "au_scaled")
                dve.wait_ge(sem("mix_done"), j + 1)
                for n in range(TB):
                    op = V.tensor_tensor(turned[:, n * P:(n + 1) * P], head_out[:, n * P:(n + 1) * P], dyn(bias_s, j),
                                         ALU.add)
                op.then_inc(sem("mix_read"), 1)
                dve.wait_ge(sem("mix_read"), j + 1)
                dve.wait_ge(sem("au_gelu"), j + 1)
                V.tensor_tensor(source[:, 1, :], k_t[:, :], turned[:, :], ALU.mult).then_inc(sem("source_ready"), 1)
                ahead(c + 3, 3)
                split_low(2 * j + 1, j, 1)

            gating(0, True)
            with dve.Fori(1, A_BLOCKS) as j:
                gating(j, False)
            dve.wait_ge(sem("positions_landed"), 16)
            chain = [0]

            def link(op):
                chain[0] += 1
                op.then_inc(sem("setup"), 1)
                dve.wait_ge(sem("setup"), chain[0])

            round_to_int = 1.5 * 2.0 ** 23
            two_pi = 2 * math.pi
            pi_high = 6.28125
            pi_mid = float(np.float32(round((two_pi - pi_high) * 2 ** 22) / 2 ** 22))
            pi_low = float(np.float32(two_pi - pi_high - pi_mid))
            limit = float(np.nextafter(np.float32(math.pi), np.float32(0)))
            link(V.tensor_copy(kw_t[:, :], gate[:, :].bitcast(I32)))
            link(V.tensor_scalar(kw_t[:, :], kw_t[:, :], column(INV_FREQ), None, ALU.mult))
            for i, (turn, shift) in enumerate(((0.25, math.pi / 2), (0.0, 0.0))):
                link(V.tensor_scalar(kr_t[:, :], kw_t[:, :], 1.0 / two_pi, turn, ALU.mult, ALU.add))
                link(V.tensor_scalar(kr_t[:, :], kr_t[:, :], round_to_int, None, ALU.add))
                link(V.tensor_scalar(kr_t[:, :], kr_t[:, :], round_to_int, None, ALU.subtract))
                link(V.scalar_tensor_tensor(out=rope2[:, i, :], in0=kr_t[:, :], scalar=-pi_high, in1=kw_t[:, :],
                                            op0=ALU.mult, op1=ALU.add))
                for part in (-pi_mid, -pi_low):
                    link(V.scalar_tensor_tensor(out=rope2[:, i, :], in0=kr_t[:, :], scalar=part, in1=rope2[:, i, :],
                                                op0=ALU.mult, op1=ALU.add))
                link(V.tensor_scalar(rope2[:, i, :], rope2[:, i, :], shift, limit, ALU.add, ALU.min))
                V.tensor_scalar(rope2[:, i, :], rope2[:, i, :], -limit, None, ALU.max).then_inc(sem("angle_ready"), 1)
            dve.wait_ge(sem("lambdas_landed"), 16)
            pairs = lam_vectors.rearrange("p l (i a f) -> p l i a f", i=2, a=2)
            products = tanh_g[:, :].rearrange("p (l i f) -> p l i f", l=LAYERS, i=2)
            for i in range(2):
                link(V.tensor_tensor(products[:, :, i], pairs[:, :, i, 0], pairs[:, :, i, 1], ALU.mult))
            V.tensor_reduce(lam_dot, tanh_g[:, :].rearrange("p (i f) -> p i f", f=64), AXIS_X, ALU.add)\
                .then_inc(sem("dots_ready"), 1)
            V.tensor_scalar(neg_sinks, col[:, SINK:SINK + 16 * LAYERS], -1.0, None, ALU.mult).then_inc(sem("sinks_ready"), 1)
            V.tensor_tensor(subln_gain, col[:, SUBLN:SUBLN + LAYERS], col[:, LAM_INIT + LAYERS:LAM_INIT + 2 * LAYERS],
                            ALU.mult).then_inc(sem("gains_ready"), 1)

            out_section(C_OUT0)
            norm(0, 1, 1, C_MLP0)
            norm_scale(2, 1, 1)
            mlp_section(C_MLP0, 16, 0)
            norm(1, 2, 3, C_QKV)
            norm_scale(4, 2, 2)
            dve.wait_ge(sem("lam_exp_ready"), 1)
            link(V.tensor_tensor(lam, lam_exp[:, 0:2 * LAYERS:2], lam_exp[:, 1:2 * LAYERS:2], ALU.subtract))
            link(V.tensor_tensor(lam, lam, col[:, LAM_INIT:LAM_INIT + LAYERS], ALU.add))
            dve.wait_ge(sem("sine_ready"), 2)
            link(V.tensor_scalar(rope2[:, 1, :], rope2[:, 1, :], column(SIGN), None, ALU.mult))
            dve.wait_ge(sem("sinks_ready"), 1)
            dve.wait_ge(sem("gains_ready"), 1)


            def scaled_tables(table, to, scale, done, count):
                for i in range(2):
                    op = V.tensor_tensor(to[:, i, :], table[:, i, :], scale, ALU.mult)
                op.then_inc(sem(done), 1)
                dve.wait_ge(sem(done), at(count))

            scaled_tables(rope1, rope_s, scale_pre[:, :], "rope1_scaled", 1)

            def dilated(i, first):
                for g in range(4):
                    hd, c = 4 * i + g, C_QKV + 12 * i + 3 * g
                    s = (3 * g) % 4
                    lone = first and g == 0

                    def free():
                        dve.wait_ge(sem("scores_done"), at(hd))
                    sum_halves(c, s)
                    rotate_cos(c, s, rope_s)
                    ahead(c, s)
                    rotate(2 * hd, 2 * hd, rope_s, q_t, free)
                    sum_halves(c + 1, (s + 1) % 4)
                    rotate_cos(c + 1, (s + 1) % 4, rope_s)
                    ahead(c + 1, (s + 1) % 4)
                    rotate(2 * hd + 1, 2 * hd + 1, rope_s, k_t, free)
                    if not lone:
                        head_low_out(hd - 1)
                    sum_halves(c + 2, (s + 2) % 4)
                    dve.wait_ge(sem("v_turned"), at(hd))
                    scale_by(v_t[:, :], c + 2, s + 2, scale_pre[:, :], "v_scaled")
                    mask_max(hd, g % 2, mask_dil, float(P) ** -0.5)
                    ahead(c + 2, (s + 2) % 4)
                    normalise(hd, g % 2)

            def head_low_out(hd):
                dve.wait_ge(sem("inner_high"), 80 + hd + 1)
                V.tensor_copy(source[:, 0, :], head_out[:, 0:TOKENS]).then_inc(sem("out_read"), 1)
                dve.wait_ge(sem("out_read"), hd + 1)
                V.tensor_tensor(dyn2(inner, hd, 1), source[:, 0, :], dyn2(inner, hd, 0), ALU.subtract)\
                    .then_inc(sem("inner_ready"), 1)

            dilated(0, True)
            with dve.Fori(1, HEADS // 4) as i:
                dilated(i, False)
            head_low_out(HEADS - 1)
            out_section(C_OUT1)
            norm(2, 3, 5, C_MLP1)
            norm_scale(6, 3, 3)
            mlp_section(C_MLP1, 96, 64)
            norm(3, 4, 7, C_LAYER2)

            with dve.Fori(0, LAYERS) as l:
                c0, u0, o0, v0, r0 = C_LAYER2 + N_LAYER2 * l, 16 + 28 * l, 16 + 16 * l, 16 + 9 * l, 8 + 8 * l
                rot0, gate0, split0, done0, sd0 = 32 + 22 * l, 16 * l, 160 + 16 * l, 16 + 24 * l, 4 + 5 * l
                cos0 = 32 + 18 * l

                norm_scale(r0, sd0, 4 + 7 * l)
                scaled_tables(rope2, rope_s, scale_pre[:, :], "rope2_scaled", l + 1)

                def gate_in(c, s, g):
                    if not isinstance(g, int) or g:
                        dve.wait_ge(sem("tanh_ready"), gate0 + g)
                    scale_by(scaled[:, 1, :], c, s, scale_pre[:, :], "gate_scaled")

                def gate_out(g):
                    dve.wait_ge(sem("tanh_ready"), gate0 + g + 1)
                    dve.wait_ge(sem("source_ready"), 144 + gate0 + g)
                    V.scalar_tensor_tensor(out=gate[:, :], in0=tanh_g[:, :], scalar=1.0, in1=scaled[:, 1, :],
                                           op0=ALU.add, op1=ALU.mult).then_inc(sem("gate_ready"), 1)

                def diff_finish(hd):
                    scale_out(r0 + 1 + hd, 5 + 7 * l + hd, scale_lat[:, 0, :])
                    V.scalar_tensor_tensor(out=normed[:, :], in0=head_out[:, 0:TOKENS], scalar=dyn_col(subln_gain, l),
                                           in1=scale_lat[:, 0, :], op0=ALU.mult, op1=ALU.mult)\
                        .then_inc(sem("out_read"), 1)
                    dve.wait_ge(sem("out_read"), o0 + hd + 1)
                    dve.wait_ge(sem("gate_ready"), gate0 + hd + 1)
                    V.scalar_tensor_tensor(out=source[:, 0, :], in0=normed[:, :], scalar=0.5, in1=gate[:, :],
                                           op0=ALU.mult, op1=ALU.mult).then_inc(sem("source_ready"), 1)

                def finish(o, g, done):
                    dve.wait_ge(sem("head_done"), done)
                    V.tensor_copy(normed[:, :], head_out[:, 0:TOKENS]).then_inc(sem("out_read"), 1)
                    dve.wait_ge(sem("out_read"), o0 + o + 1)
                    dve.wait_ge(sem("gate_ready"), gate0 + g + 1)
                    V.scalar_tensor_tensor(out=source[:, 0, :], in0=normed[:, :], scalar=0.5, in1=gate[:, :],
                                           op0=ALU.mult, op1=ALU.mult).then_inc(sem("source_ready"), 1)

                def combine(hd):
                    u = u0 + 2 * hd
                    dve.wait_ge(sem("exp_ready"), 2 * u + 4)
                    V.reciprocal(small[:, 8:12], small[:, 4:8]).then_inc(sem("inverse_ready"), 2)
                    dve.wait_ge(sem("inverse_ready"), u + 2)
                    V.tensor_scalar(inverse(1), inverse(1), dyn_col(lam, l), None, ALU.mult).then_inc(sem("lam_inverse"), 1)
                    dve.wait_ge(sem("lam_inverse"), DA_HEADS * l + hd + 1)
                    for t, (lo, hi) in enumerate(((0, P), (P, COLS))):
                        op = V.tensor_scalar(prob[:, 1, lo:hi], prob[:, 1, lo:hi], inverse(1, t), None, ALU.mult)
                    op.then_inc(sem("second_scaled"), 1)
                    dve.wait_ge(sem("second_scaled"), DA_HEADS * l + hd + 1)
                    for t, (lo, hi) in enumerate(((0, P), (P, COLS))):
                        op = V.scalar_tensor_tensor(out=prob[:, 0, lo:hi], in0=prob[:, 0, lo:hi], scalar=inverse(0, t),
                                                    in1=prob[:, 1, lo:hi], op0=ALU.mult, op1=ALU.subtract)
                    op.then_inc(sem("prob_ready"), 2)

                def diff_mean(hd):
                    mean(r0 + 1 + hd, P, SUBLN_EPS, "stat_done", sd0 + hd + 2)

                def differential(hd, first):
                    c = c0 + 4 * hd

                    def free():
                        dve.wait_ge(sem("scores_done"), u0 + 2 * hd)
                    sum_halves(c, 0)
                    rotate_cos(c, 0, rope_s)
                    ahead(c, 0)
                    rotate(rot0 + 2 * hd, cos0 + 2 * hd, rope_s, q_t, free)
                    sum_halves(c + 1, 1)
                    rotate_cos(c + 1, 1, rope_s)
                    ahead(c + 1, 1)
                    rotate(rot0 + 2 * hd + 1, cos0 + 2 * hd + 1, rope_s, k_t, free)
                    sum_halves(c + 2, 2)
                    dve.wait_ge(sem("v_turned"), v0 + hd)
                    scale_by(v_t[:, :], c + 2, 2, scale_pre[:, :], "v_scaled")
                    for j in range(2):
                        mask_max(u0 + 2 * hd + j, j, mask_causal, 64.0 ** -0.5)
                    ahead(c + 2, 2)
                    if not first:
                        diff_mean(hd - 1)
                    sum_halves(c + 3, 3)
                    gate_in(c + 3, 3, hd)
                    if not first:
                        diff_finish(hd - 1)
                    gate_out(hd)
                    combine(hd)
                    ahead(c + 3, 3)
                    if not first:
                        split_low(split0 + hd - 1, hd - 1, 0)

                differential(0, True)
                with dve.Fori(1, DA_HEADS) as hd:
                    differential(hd, False)

                c, hd = c0 + N_DA, DA_HEADS - 1

                def all_scored():
                    dve.wait_ge(sem("scores_done"), u0)
                sum_halves(c, 0)
                rotate_cos(c, 0, rope_s)
                ahead(c, 0, units=1)
                rotate(rot0 + 8, cos0 + 8, rope_s, kw_t, all_scored)
                sum_halves(c + 1, 1)
                dve.wait_ge(sem("v_turned"), v0 + DA_HEADS)
                scale_by(v_t[:, :], c + 1, 1, scale_pre[:, :], "v_scaled")
                ahead(c + 1, 1)
                sum_halves(c + 2, 2)
                rotate_cos(c + 2, 2, rope_s)
                ahead(c + 2, 2)
                rotate(rot0 + 9, cos0 + 9, rope_s, kr_t, all_scored)
                diff_mean(hd)
                sum_halves(c + 3, 3)
                dve.wait_ge(sem("v_ready"), v0 + DA_HEADS + 1)
                diff_finish(hd)
                ahead(c + 3, 3)
                split_low(split0 + hd, hd, 0)

                def window(i, first):
                    for g in range(2):
                        b, c = 2 * i + g, c0 + N_DA + N_KV + 4 * i + 2 * g
                        lone = first and g == 0

                        def free():
                            dve.wait_ge(sem("scores_done"), u0 + 8 + 2 * b)
                        sum_halves(c, 2 * g)
                        rotate_cos(c, 2 * g, rope_s)
                        ahead(c, 2 * g)
                        rotate(rot0 + 10 + b, cos0 + 10 + b, rope_s, q_t, free)
                        sum_halves(c + 1, 2 * g + 1)
                        gate_in(c + 1, 1, DA_HEADS + b)
                        if not lone:
                            finish(DA_HEADS + b - 1, DA_HEADS + b - 1, done0 + DA_HEADS + 2 * b)
                        gate_out(DA_HEADS + b)
                        for j in range(2):
                            mask_max(u0 + 8 + 2 * b + j, j, mask_window, 64.0 ** -0.5,
                                     neg_sink=(dyn_col(neg_sinks, 16 * l + 8 * j + b), 16 * l + 2 * b + j))
                        ahead(c + 1, 2 * g + 1)
                        for j in range(2):
                            normalise(u0 + 8 + 2 * b + j, j, sink=16 * l + 2 * b + j)
                        if not lone:
                            split_low(split0 + DA_HEADS + b - 1, DA_HEADS + b - 1, 0)

                window(0, True)
                with dve.Fori(1, SW_BLOCKS // 2) as i:
                    window(i, False)

                c = c0 + N_DA + N_KV + N_SW
                for i in range(N_LATENT):
                    sum_halves(c + i, i % 4)
                    if i > 1:
                        dve.wait_ge(sem("latent_squared"), N_LATENT * l + i - 1)
                    if i < 2:
                        dve.wait_ge(sem("tanh_ready"), gate0 + 12)
                    scale_by(scaled[:, i % 2, :], c + i, i, scale_pre[:, :], "latent_scaled")
                    if i == 1:
                        finish(11, 11, done0 + DA_HEADS + 2 * SW_BLOCKS)
                    ahead(c + i, i % 4)
                    dve.wait_ge(sem("latent_high"), N_LATENT * l + i + 1)
                    dve.wait_ge(sem("latent_scaled"), N_LATENT * l + i + 1)
                    V.scalar_tensor_tensor(out=latent[:, i, 1, :], in0=scaled[:, i % 2, :], scalar=latent_gain(l, i),
                                           in1=latent[:, i, 0, :], op0=ALU.mult, op1=ALU.subtract)\
                        .then_inc(sem("latent_ready"), 1)
                    if i == 1:
                        split_low(split0 + 11, 11, 0)
                    if i == LATENT:
                        mean(r0 + 5, LATENT * P, NORM_EPS, "latent_counted", N_LATENT * l + LATENT)
                    if i == LATENT + 1:
                        scale_out(r0 + 5, 9 + 7 * l, scale_lat[:, 0, :])
                        scaled_tables(rope2, rope_q, scale_lat[:, 0, :], "rope_q_scaled", l + 1)

                c = c + N_LATENT
                for hd in range(MLA_HEADS):
                    s = (2 * hd) % 4
                    s2 = (s + 2) % 4
                    if hd == 0:
                        mean(r0 + 6, LATENT * P, NORM_EPS, "latent_counted", N_LATENT * (l + 1))
                        scale_out(r0 + 6, 10 + 7 * l, scale_lat[:, 1, :])
                    dve.wait_ge(corr_ready, c + 2 * hd + 1)
                    dve.wait_ge(sem("swapped_ready"), rot0 + 19 + hd)
                    dve.wait_ge(sem("scores_done"), u0 + 24 + hd)
                    dve.wait_ge(sem("v_turned"), v0 + 5 + hd)
                    V.tensor_tensor(v_t[:, :], acc[s2][:, 0:TOKENS], scale_lat[:, 1, :], ALU.mult)\
                        .then_inc(sem("v_scaled"), 1)
                    V.tensor_tensor(q_t[:, :], acc[s][:, 0:TOKENS], scale_lat[:, 0, :], ALU.mult)
                    V.tensor_tensor(k_t[:, :], acc[s][:, TOKENS:], scale_lat[:, 1, :], ALU.mult)\
                        .then_inc(sem("nope_ready"), 1)
                    V.tensor_tensor(scaled[:, 0, :], corr[:, 0, :], rope_q[:, 0, :], ALU.mult).then_inc(summed, 1)
                    dve.wait_ge(summed, c + 2 * hd + 1)
                    V.tensor_tensor(turned[:, :], swapped[:, :], rope_q[:, 1, :], ALU.mult).then_inc(sem("rot_sin"), 1)
                    dve.wait_ge(sem("rot_sin"), rot0 + 19 + hd)
                    V.tensor_tensor(qr_t[:, :], scaled[:, 0, :], turned[:, :], ALU.add).then_inc(sem("rotated"), 1)
                    ahead(c + 2 * hd, s)
                    sum_halves(c + 2 * hd + 1, s + 1)
                    gate_in(c + 2 * hd + 1, 1, 12 + hd)
                    if hd:
                        finish(11 + hd, 11 + hd, done0 + 20 + hd)
                    gate_out(12 + hd)
                    mask_max(u0 + 24 + hd, hd % 2, mask_causal, 192.0 ** -0.5)
                    ahead(c + 2 * hd + 1, s + 1)
                    normalise(u0 + 24 + hd, hd % 2)
                    if hd:
                        split_low(split0 + 11 + hd, 11 + hd, 0)
                finish(15, 15, done0 + 24)
                split_low(split0 + 15, 15, 0)
                out_section(c + N_MLA)
                norm(4 + l, 5 + l, r0 + 7, c0 + N_LAYER2)


def weight_stream(w_in_ab, w_out_ab, w_qkv, w_o, w_up, w_down, w_in_2, w_uq_2, w_ukv_2, w_out_2):
    stream = np.zeros((LOADED, P, UNITS, P), np.float32)
    at = [0]

    def put(columns):
        stream[at[0]] = columns.reshape(UNITS, P, P).transpose(1, 0, 2)
        at[0] += 1

    def blocks(w, first, count=1, width=P):
        for i in range(count):
            put(w[:, first + width * i:first + width * (i + 1)])

    w = w_in_ab[0]
    width = A_BLOCKS * P
    blocks(w, width, A_BLOCKS)
    for j in range(A_BLOCKS):
        for part in (3, 4, 2, 0):
            blocks(w, part * width + P * j)
    blocks(w_out_ab[0], 0, KB)

    def mlp(layer):
        for q in range(FFN_QUARTERS):
            blocks(w_up[layer], D * q, KB)
            blocks(w_down[layer][D * q:D * (q + 1)], 0, KB)

    mlp(0)
    for hd in range(HEADS):
        for part in range(3):
            blocks(w_qkv[0], D * part + P * hd)
    blocks(w_o[0], 0, KB)
    mlp(1)

    half = P // 2
    for layer in range(LAYERS):
        w = w_in_2[layer]
        for hd in range(DA_HEADS):
            for first in (0, 512, 1024, 1536):
                blocks(w, first + P * hd)
        blocks(w, 3072)
        blocks(w, 3200)
        put(np.concatenate([w[:, 5376:5440]] * 2, 1))
        at[0] += 1
        for b in range(SW_BLOCKS):
            for first in (2048, 3328):
                put(np.concatenate([w[:, first + half * b:first + half * (b + 1)],
                                    w[:, first + half * (8 + b):first + half * (9 + b)]], 1))
        blocks(w, 4352, LATENT)
        blocks(w, 4864, LATENT)
        uq, ukv = w_uq_2[layer], w_ukv_2[layer]
        for hd in range(MLA_HEADS):
            pair = [192 * (2 * (hd // 2) + i) + P for i in range(2)]
            put(np.concatenate([uq[:, 192 * hd:192 * hd + P], ukv[:, 256 * hd:256 * hd + P],
                                ukv[:, 256 * hd + P:256 * (hd + 1)],
                                np.concatenate([uq[:, a:a + half] for a in pair], 1)]))
            blocks(w, 5440 + P * hd)
        order = list(range(512))
        for b in range(SW_BLOCKS):
            for first in (512 + half * b, 512 + half * (8 + b)):
                order += list(range(first, first + half))
        order += list(range(1536, D))
        blocks(w_out_2[layer][order], 0, KB)
    return stream.reshape(LOADED, P, UNITS * P)


def per_feature(sink_logits_2, gains_pre, gains_post, conv_w, q_norm, kv_norm, subln):
    col = np.zeros((P, N_COLS), np.float32)
    for i, g in enumerate(gains_pre):
        col[:, G_PRE + KB * i:G_PRE + KB * (i + 1)] = g.reshape(KB, P).T
    for i, g in enumerate(gains_post):
        col[:, G_POST + KB * i:G_POST + KB * (i + 1)] = g.reshape(KB, P).T
    col[:, CONV:CONV + 3 * A_BLOCKS] = conv_w[0].reshape(3 * A_BLOCKS, P).T
    col[:, Q_NORM:Q_NORM + LAYERS * LATENT] = q_norm.reshape(LAYERS * LATENT, P).T
    col[:, KV_NORM:KV_NORM + LAYERS * LATENT] = kv_norm.reshape(LAYERS * LATENT, P).T
    col[:, SUBLN:SUBLN + LAYERS] = subln.T
    col[:, SINK:SINK + 16 * LAYERS] = sink_logits_2.reshape(1, -1)
    p = np.arange(P)
    col[:, INV_FREQ] = (10000.0 ** (-(p % 32) * 2.0 / 64)).astype(np.float32)
    col[:, SIGN] = np.where(p % 64 < 32, -1, 1)
    for layer in range(LAYERS):
        lam_init = 0.8 - 0.6 * math.exp(-0.3 * layer)
        col[:, LAM_INIT + layer] = lam_init
        col[:, LAM_INIT + LAYERS + layer] = 1 - lam_init
    return col


def shape_tables():
    t, s = np.arange(TOKENS)[:, None], np.arange(TOKENS)[None, :]
    back = t - s
    count = sum(((back >= 0) & (back % dilation == 0) & (back // dilation <= window // dilation)).astype(int)
                for window, dilation in ((128, 1), (512, 4), (2048, 16)))
    masks = [np.where(count > 0, np.log(np.maximum(count, 1)), MASKED), np.where(back >= 0, 0, MASKED),
             np.where((back >= 0) & (back < 128), 0, MASKED)]
    parts = [np.eye(P), np.ones((P, P))]
    for m in masks:
        parts += [m[:P, :P], m[P:, :]]
    half = P // 2
    freq = np.float32(10000.0) ** (-np.arange(half, dtype=np.float32) * np.float32(2.0) / np.float32(P))
    angle = (np.arange(TOKENS, dtype=np.float32)[None, :] * freq.astype(np.float32)[:, None]).astype(np.float64)
    parts += [np.concatenate([np.cos(angle)] * 2), np.concatenate([-np.sin(angle), np.sin(angle)])]
    return np.ascontiguousarray(np.concatenate(parts, 1).astype(np.float32))


def kernel(x, norm_mix_pre, norm_mix_post, norm_mlp_pre, norm_mlp_post, w_in_ab, w_spatial, b_spatial,
           conv_w, w_out_ab, w_qkv, w_o, w_up, w_down, positions_2, pre_norm_w_2, post_norm_w_2,
           w_in_2, diff_lambda_q1_2, diff_lambda_k1_2, diff_lambda_q2_2, diff_lambda_k2_2,
           diff_subln_w_2, sink_logits_2, mla_q_norm_w_2, mla_kv_norm_w_2, w_uq_2, w_ukv_2, w_out_2):
    import concourse.bacc as _bacc
    from concourse.bass_utils import run_bass_kernel_spmd as _run

    gains_pre = [norm_mix_pre[0], norm_mlp_pre[0], norm_mix_pre[1], norm_mlp_pre[1], *pre_norm_w_2]
    gains_post = [norm_mix_post[0], norm_mlp_post[0], norm_mix_post[1], norm_mlp_post[1], *post_norm_w_2]
    lambdas = np.stack([diff_lambda_q1_2, diff_lambda_k1_2, diff_lambda_q2_2, diff_lambda_k2_2], 1)
    arrays = {
        "stream": weight_stream(w_in_ab, w_out_ab, w_qkv, w_o, w_up, w_down, w_in_2, w_uq_2, w_ukv_2, w_out_2),
        "x_t": np.ascontiguousarray(x[0].T.reshape(KB, P, TOKENS).transpose(1, 0, 2)),
        "columns": per_feature(sink_logits_2, gains_pre, gains_post, conv_w, mla_q_norm_w_2, mla_kv_norm_w_2,
                               diff_subln_w_2),
        "lambdas": np.ascontiguousarray(np.broadcast_to(lambdas.reshape(1, LAYERS, 256), (P, LAYERS, 256))),
        "w_spatial": np.ascontiguousarray(w_spatial[0].transpose(2, 0, 1)),
        "b_spatial": np.ascontiguousarray(np.broadcast_to(b_spatial, (P, A_BLOCKS, P))),
        "positions": np.ascontiguousarray(np.broadcast_to(positions_2, (P, TOKENS))),
        "tables": shape_tables(),
    }
    nc = _bacc.Bacc("TRN2", target_bir_lowering=False, num_devices=1)
    args = [nc.dram_tensor(name, a.shape, mybir.dt.from_np(a.dtype), kind="ExternalInput").ap()
            for name, a in arrays.items()]
    args.append(nc.dram_tensor("out_0", (P, KB, TOKENS), F32, kind="ExternalOutput").ap())
    build(nc, *args)
    r = _run(nc, [arrays], core_ids=[0])
    return r.results[0]["out_0"].transpose(2, 1, 0).reshape(1, TOKENS, D)
```

```python
import math

import numpy as np

import concourse.bass as bass
from concourse import mybir
from contextlib import ExitStack

F32 = mybir.dt.float32
F32R = mybir.dt.float32r
I32 = mybir.dt.int32
ACT = mybir.ActivationFunctionType
ALU = mybir.AluOpType
AXIS_X = mybir.AxisListType.X

P = 128
TOKENS = 256
TB = TOKENS // P
D = 2048
KB = D // P
UNITS = 16
LAYERS = 2

A_BLOCKS = 8
HEADS = 16
FFN_QUARTERS = 4
DA_HEADS, SW_BLOCKS, MLA_HEADS = 4, 8, 4
N_MIX0 = 5 * A_BLOCKS
N_OUT = KB
N_MLP = FFN_QUARTERS * 2 * KB
N_QKV = 3 * HEADS
N_DA = 4 * DA_HEADS
N_KV = 4
N_SW = 2 * SW_BLOCKS
N_LATENT = 8
N_MLA = 2 * MLA_HEADS
N_LAYER2 = N_DA + N_KV + N_SW + N_LATENT + N_MLA + N_OUT
C_MIX0 = 0
C_OUT0 = C_MIX0 + N_MIX0
C_MLP0 = C_OUT0 + N_OUT
C_QKV = C_MLP0 + N_MLP
C_OUT1 = C_QKV + N_QKV
C_MLP1 = C_OUT1 + N_OUT
C_LAYER2 = C_MLP1 + N_MLP
CHUNKS = C_LAYER2 + LAYERS * N_LAYER2
AHEAD = 3
LOADED = CHUNKS + AHEAD

NORM_EPS = 1e-6
LN_EPS = 1e-5
SUBLN_EPS = 1e-5
MASKED = -1e30
NORM_GROUPS = [(0, 1), (1, 1)] + [(b, 2) for b in range(2, KB, 2)]
FIRST_SPLITS = [2, 8]
STAT_AT, SPREAD_AT = 0, 8
LATE = 4
LATENT = 4
COLS = 3 * P

NORMS = 6
G_PRE = 0
G_POST = G_PRE + NORMS * KB
CONV = G_POST + NORMS * KB
Q_NORM = CONV + 3 * A_BLOCKS
KV_NORM = Q_NORM + LAYERS * LATENT
SUBLN = KV_NORM + LAYERS * LATENT
SINK = SUBLN + LAYERS
INV_FREQ = SINK + LAYERS * 16
SIGN = INV_FREQ + 1
LAM_INIT = SIGN + 1
N_COLS = LAM_INIT + 2 * LAYERS


def squares_pre(n):
    return 2 * KB * n


def squares_post(n):
    return 2 * KB * n + KB


def build(nc, stream, x_t, columns, lambdas, w_spatial, b_spatial, positions, tables, out):
    ctx = ExitStack()
    with ctx:
        def sb(name, shape, dt=F32):
            return ctx.enter_context(nc.sbuf_tensor(name, shape, dt))

        sems = {}

        def sem(name):
            if name not in sems:
                sems[name] = ctx.enter_context(nc.semaphore(name))
            return sems[name]

        with nc.sbuf_tensor("raw", [P, 4, UNITS * P], F32) as raw:
            pass
        w_low = sb("w_low", [P, 4, UNITS * P], F32R)
        w_high = sb("w_high", [P, 4, UNITS * P], F32R)
        xs = sb("xs", [P, KB, 2, TOKENS], F32R)
        inner = sb("inner", [P, KB, 2, TOKENS], F32R)
        h = sb("h", [P, KB, TOKENS])
        with nc.sbuf_tensor("branch", [P, KB, TOKENS], F32) as branch:
            pass
        with nc.sbuf_tensor("latent", [P, 2 * LATENT, 2, TOKENS], F32R) as latent:
            pass
        sb("branch_or_latent", [P, KB, TOKENS])
        a_v = branch[:, 0:8, :].rearrange("p a b -> p (a b)").rearrange("p (n f) -> p n f", n=TB)
        spatial = branch[:, 8:12, :].rearrange("p a b -> p (a b)").rearrange("p (g t) -> p g t", g=A_BLOCKS)
        bias_s = branch[:, 12:16, :].rearrange("p a b -> p (a b)").rearrange("p (g t) -> p g t", g=A_BLOCKS)

        col = sb("col", [P, N_COLS])
        consts = sb("consts", [P, 2 * P + 3 * COLS + 2 * TOKENS])
        ident = consts[:, 0:P]
        ones = consts[:, P:2 * P]
        mask_dil = consts[:, 2 * P:2 * P + COLS]
        mask_causal = consts[:, 2 * P + COLS:2 * P + 2 * COLS]
        mask_window = consts[:, 2 * P + 2 * COLS:2 * P + 3 * COLS]
        rope1 = consts[:, 2 * P + 3 * COLS:].rearrange("p (a t) -> p a t", a=2)
        rope_q = rope1
        rope2 = sb("rope2", [P, 2, TOKENS])
        rope_s = sb("rope_s", [P, 2, TOKENS])
        corr = sb("corr", [P, 2, TOKENS])
        y = sb("y", [P, 2, TOKENS])
        scaled = sb("scaled", [P, 2, TOKENS])
        source = sb("source", [P, 2, TOKENS])
        sq = sb("sq", [P, 2, TOKENS])
        sum_sq = sb("sum_sq", [P, TOKENS])
        step = sb("step", [P, 2, TOKENS])
        latent_sq = step
        head_sq = step[:, 0, :]
        scale_pre = sb("scale_pre", [P, TOKENS])
        scale_lat = sb("scale_lat", [P, 2, TOKENS])
        swapped = sb("swapped", [P, TOKENS])
        turned = sb("turned", [P, TOKENS])
        q_t = sb("q_t", [P, TOKENS])
        k_t = sb("k_t", [P, TOKENS])
        v_t = sb("v_t", [P, TOKENS])
        v_nat = sb("v_nat", [P, TB, P])
        kw_t = sb("kw_t", [P, TOKENS])
        vw_nat = sb("vw_nat", [P, TB, P])
        kr_t = sb("kr_t", [P, TOKENS])
        qr_t = kw_t
        gate = sb("gate", [P, TOKENS])
        tanh_g = sb("tanh_g", [P, TOKENS])
        normed = source[:, 1, :]
        diag = sb("diag", [P, TOKENS])
        prob = sb("prob", [P, 2, COLS])
        prob_t = sb("prob_t", [P, 2, COLS])
        conv_in = prob[:, 0, 0:TOKENS + 2]
        bn = prob[:, 1, 0:TB * 12].rearrange("p (n k f) -> p n k f", n=TB, k=2)
        lam_vectors = prob_t[:, :, 0:256]
        small = sb("small", [P, 72])
        minus_half = sb("minus_half", [P, TB])

        def neg_max(bank, t=None):
            return small[:, 2 * bank:2 * bank + 2] if t is None else small[:, 2 * bank + t:2 * bank + t + 1]

        def denom(bank, t=None):
            return small[:, 4 + 2 * bank:6 + 2 * bank] if t is None else small[:, 4 + 2 * bank + t:5 + 2 * bank + t]

        def inverse(bank, t=None):
            return small[:, 8 + 2 * bank:10 + 2 * bank] if t is None else small[:, 8 + 2 * bank + t:9 + 2 * bank + t]

        def exp_sink(bank):
            return small[:, 12 + 2 * bank:14 + 2 * bank]

        mean_of, root_of = small[:, 16:18], small[:, 18:20]
        av_moments, av_var, av_root = small[:, 20:24], small[:, 24:26], small[:, 26:28]
        lam_dot, lam_exp, lam = small[:, 28:32], small[:, 32:36], small[:, 36:38]
        subln_gain, neg_sinks = small[:, 38:40], small[:, 40:72]

        def psum_bank(name):
            return ctx.enter_context(nc.psum_tensor(name, [P, 512], F32))

        acc = [psum_bank(f"acc{i}") for i in range(4)]
        score = [psum_bank(f"score{i}") for i in range(2)]
        head_out = psum_bank("head_out")
        extra = psum_bank("extra")

        landed = [sem(f"landed_{s}") for s in range(4)]
        high_ready, low_ready = sem("high_ready"), sem("low_ready")
        product_done, corr_ready, summed = sem("product_done"), sem("corr_ready"), sem("summed")

        def dyn(t, i):
            return t[:, i] if isinstance(i, int) else t[:, bass.ds(i, 1)].rearrange("p a b -> p (a b)")

        def dyn2(t, i, part):
            if isinstance(i, int):
                return t[:, i, part]
            return t[:, bass.ds(i, 1), part].rearrange("p a b -> p (a b)")

        def dyn_col(t, i):
            return t[:, i:i + 1] if isinstance(i, int) else t[:, bass.ds(i, 1)]

        def column(i):
            return dyn_col(col, i)

        def latent_gain(l, i):
            return column((Q_NORM if i < LATENT else KV_NORM - LATENT) + i + LATENT * l)

        def at(value):
            return max(value, 0) if isinstance(value, int) else value

        block = ctx.enter_context(nc.Block())

        @block.sync
        def _(sp):
            def load(c, s):
                sp.dma_start(raw[:, s, :], stream[c] if isinstance(c, int)
                             else stream[bass.ds(c, 1)].rearrange("a p n -> (a p) n")).then_inc(landed[s], 16)

            sp.dma_start(col[:, :], columns).then_inc(sem("columns_landed"), 16)
            for part in range(4):
                b = part * KB // 4
                sp.dma_start(h[:, b:b + KB // 4, :], x_t[:, b:b + KB // 4, :]).then_inc(sem(f"x_landed_{part}"), 16)
                if part == 0:
                    load(0, 0)
            for s in range(1, 4):
                load(s, s)
            sp.dma_start(consts[:, :], tables).then_inc(sem("tables_landed"), 16)
            sp.dma_start(spatial, w_spatial).then_inc(sem("spatial_landed"), 16)
            sp.dma_start(bias_s, b_spatial).then_inc(sem("bias_landed"), 16)
            sp.dma_start(gate[:, :].bitcast(I32), positions).then_inc(sem("positions_landed"), 16)
            sp.dma_start(lam_vectors, lambdas).then_inc(sem("lambdas_landed"), 16)
            with sp.Fori(1, LOADED // 4) as i:
                for s in range(4):
                    sp.wait_ge(product_done, 4 * i + (s - 3))
                    load(4 * i + s, s)
            for c in range(LOADED - LOADED % 4, LOADED):
                sp.wait_ge(product_done, c - 3)
                load(c, c % 4)
            for part in range(4):
                b = part * KB // 4
                sp.wait_ge(sem("h_ready"), KB * (NORMS - 1) + b + KB // 4)
                sp.dma_start(out[:, b:b + KB // 4, :], h[:, b:b + KB // 4, :]).then_inc(sem("out_written"), 16)
            sp.wait_ge(sem("out_written"), 4 * 16)

        @block.tensor
        def _(pe):
            def high_unit(s, kt, x):
                nc.tensor.matmul(acc[s][:, :], w_high[:, s, kt * P:(kt + 1) * P], x[:, kt, :, :],
                                 start=(kt == first_of[0]), stop=False, skip_group_check=True)

            first_of = [0]

            def low_unit(s, kt, x, stop):
                return nc.tensor.matmul(acc[s][:, TOKENS:], w_low[:, s, kt * P:(kt + 1) * P], x[:, kt, 0, :],
                                        start=False, stop=stop, skip_group_check=True)

            def product(c, s, x, units=UNITS, ready=None, hooks=None):
                pe.wait_ge(high_ready, c + 1)
                pe.wait_ge(summed, at(c - 3))
                first_of[0] = 0
                for kt in range(units):
                    if hooks and kt in hooks:
                        hooks[kt]()
                    if ready:
                        ready(kt)
                    high_unit(s, kt, x)
                pe.wait_ge(low_ready, c + 1)
                for kt in range(units):
                    mm = low_unit(s, kt, x, kt == units - 1)
                mm.then_inc(product_done, 1)

            def product_first(c, n):
                pe.wait_ge(high_ready, c + 3)
                pe.wait_ge(low_ready, c + 3)
                pe.wait_ge(summed, at(c))
                first_of[0] = 0
                for kt in range(KB):
                    pe.wait_ge(sem("xs_ready"), KB * n + kt + 1)
                    for s in range(3):
                        high_unit(s, kt, xs)
                        mm = low_unit(s, kt, xs, kt == KB - 1)
                        if kt == KB - 1:
                            mm.then_inc(product_done, 1)

            def product_early(c, split0, late, order=None, hooks=None):
                order = order or list(range(KB))
                early = KB - late
                first_of[0] = order[0]
                for s in range(3):
                    pe.wait_ge(high_ready, c + s + 1)
                    pe.wait_ge(summed, c + s - 3)
                    for i, kt in enumerate(order[:early]):
                        if hooks and early * s + i in hooks:
                            hooks[early * s + i]()
                        if s == 0:
                            pe.wait_ge(sem("inner_ready"), split0 + i + 1)
                        high_unit(s, kt, inner)
                for s in range(3):
                    for i, kt in enumerate(order[early:]):
                        if s == 0:
                            pe.wait_ge(sem("inner_ready"), split0 + early + i + 1)
                        high_unit(s, kt, inner)
                    pe.wait_ge(low_ready, c + s + 1)
                    for kt in range(KB):
                        mm = low_unit(s, kt, inner, kt == KB - 1)
                    mm.then_inc(product_done, 1)

            def sum_over_features(parts, done):
                for i, part in enumerate(parts):
                    for n in range(TB):
                        mm = nc.tensor.matmul(extra[:, TOKENS + n:TOKENS + n + 1], part[:, n * P:(n + 1) * P],
                                              ones[:, 0:1], start=(i == 0 and n == 0), stop=(i == len(parts) - 1),
                                              skip_group_check=True)
                mm.then_inc(sem(done), 1)

            def spread(r):
                pe.wait_ge(sem("diag_ready"), r + 1)
                nc.tensor.matmul(extra[:, 0:TOKENS], ones, diag[:, :], start=True, stop=True)\
                    .then_inc(sem("spread_done"), 1)

            def stat_pre(n, copied):
                pe.wait_ge(sem("scale_ready"), at(copied))
                pe.wait_ge(sem("square_added"), squares_pre(n) + KB)
                sum_over_features([sum_sq[:, :]], "stat_done")

            def stat_post(m, r):
                pe.wait_ge(sem("square_added"), squares_post(m) + KB - 1)
                pe.wait_ge(sem("squared"), squares_post(m) + KB)
                sum_over_features([sum_sq[:, :], sq[:, 1, :]], "square_added")
                spread(r)

            def scores(u, bank, pairs, q_ready):
                q_ready()
                pe.wait_ge(sem("prob_t_ready"), at(u - 1))
                for (lo, hi, t0) in ((0, P, 0), (P, COLS, P)):
                    for i, (q, k) in enumerate(pairs):
                        mm = nc.tensor.matmul(score[bank][:, lo:hi], q[:, t0:t0 + P], k[:, 0:hi - lo],
                                              start=(i == 0), stop=(i == len(pairs) - 1))
                mm.then_inc(sem("scores_done"), 1)

            def turn_prob(u, bank, count=1):
                pe.wait_ge(sem("prob_ready"), u + count)
                for lo, to in ((0, 0), (P, P), (2 * P, 2 * P)):
                    mm = nc.tensor.transpose(score[bank][:, to:to + P], prob[:, bank, lo:lo + P], ident)
                mm.then_inc(sem("prob_turned"), count)

            def turn_value(v, o):
                pe.wait_ge(sem("v_scaled"), v + 1)
                pe.wait_ge(sem("out_read"), at(o))
                for n in range(TB):
                    mm = nc.tensor.transpose(head_out[:, TOKENS + n * P:TOKENS + (n + 1) * P],
                                             v_t[:, n * P:(n + 1) * P], ident)
                mm.then_inc(sem("v_turned"), 1)

            def weigh(u, bank, values, o, v=None, part=(0, P), count=1, last=True):
                pe.wait_ge(sem("prob_t_ready"), u + count)
                if v is not None:
                    pe.wait_ge(sem("v_ready"), v + 1)
                pe.wait_ge(sem("out_read"), at(o))
                a, b = part
                nc.tensor.matmul(head_out[a:b, 0:TOKENS], values[:, 0, a:b], prob_t[:, bank, 0:TOKENS],
                                 start=True, stop=False, skip_group_check=True)
                mm = nc.tensor.matmul(head_out[a:b, P:TOKENS], values[:, 1, a:b], prob_t[:, bank, TOKENS:COLS],
                                      start=False, stop=True, skip_group_check=True)
                mm.then_inc(sem("head_done"), 1)

            def out_section(c0, split0, late, order=None, hooks=None):
                product_early(c0, split0, late, order, hooks)
                product(c0 + 3, 3, inner)
                with pe.Fori(1, KB // 4) as i:
                    for s in range(4):
                        product(c0 + 4 * i + s, s, inner)

            def mlp_section(c0, split0, n, r):
                def quarter(q, first):
                    c = c0 + 2 * KB * q
                    if first:
                        product_first(c, n)
                        product(c + 3, 3, xs, hooks={STAT_AT: lambda: stat_pre(n, n), SPREAD_AT: lambda: spread(r)})
                    with pe.Fori(int(first), KB // 4) as i:
                        for s in range(4):
                            product(c + 4 * i + s, s, xs)
                    c = c + KB
                    product_early(c, split0 + KB * q, LATE)
                    product(c + 3, 3, inner)
                    with pe.Fori(1, KB // 4) as i:
                        for s in range(4):
                            product(c + 4 * i + s, s, inner)
                quarter(0, True)
                with pe.Fori(1, FFN_QUARTERS) as q:
                    quarter(q, False)

            product(0, 0, xs, ready=lambda kt: pe.wait_ge(sem("xs_ready"), kt + 1))
            product(1, 1, xs)
            pe.wait_ge(sem("tables_landed"), 16)
            product(2, 2, xs, hooks={12: lambda: stat_pre(0, 0)})

            def turn_av(j):
                pe.wait_ge(sem("av_gelu"), j + 1)
                pe.wait_ge(sem("av_copied"), at(j))
                for n in range(TB):
                    mm = nc.tensor.transpose(head_out[:, n * P:(n + 1) * P], (q_t, k_t)[j % 2][:, n * P:(n + 1) * P],
                                             ident)
                mm.then_inc(sem("av_turned"), 1)

            product(3, 3, xs, hooks={4: lambda: spread(0)})
            for j in range(3):
                turn_av(j)
            for j in range(4, A_BLOCKS):
                product(j, j % 4, xs)
                turn_av(j - 1)

            def mix(j):
                pe.wait_ge(sem("av_staged"), j + 1)
                pe.wait_ge(sem("mix_read"), at(j))
                for n in range(TB):
                    mm = nc.tensor.matmul(head_out[:, n * P:(n + 1) * P], v_nat[:, n, :], dyn(spatial, j),
                                          start=True, stop=True, skip_group_check=True)
                mm.then_inc(sem("mix_done"), 1)

            def gating(j, first):
                c = A_BLOCKS + 4 * j
                product(c, 0, xs)
                if first:
                    turn_av(A_BLOCKS - 1)
                    pe.wait_ge(sem("spatial_ready"), 1)
                product(c + 1, 1, xs)
                product(c + 2, 2, xs)
                product(c + 3, 3, xs, hooks={12: lambda: mix(j)})

            gating(0, True)
            with pe.Fori(1, A_BLOCKS) as j:
                gating(j, False)
            out_section(C_OUT0, 0, 2, order=[b for j in range(A_BLOCKS) for b in (A_BLOCKS + j, j)])
            stat_post(0, 1)
            mlp_section(C_MLP0, 16, 1, 2)
            stat_post(1, 3)

            def dilated_scores(hd, bank):
                def ready():
                    pe.wait_ge(sem("rotated"), 2 * hd + 2)
                scores(hd, bank, [(q_t, k_t)], ready)

            def dilated(i, first):
                for g in range(4):
                    hd, c = 4 * i + g, C_QKV + 12 * i + 3 * g
                    s = (3 * g) % 4
                    lone = first and g == 0
                    if lone:
                        product_first(c, 2)
                        product(c + 3, 3, xs, hooks={STAT_AT: lambda: stat_pre(2, 2), SPREAD_AT: lambda: spread(4)})
                        continue
                    second = first and g == 1
                    if not second:
                        product(c, s, xs)
                        turn_value(hd - 1, hd - 1)
                        turn_prob(hd - 1, (g - 1) % 2)
                    product(c + 1, (s + 1) % 4, xs, hooks={8: lambda: dilated_scores(0, 0)} if second else None)

                    def turns():
                        turn_value(0, 0)
                        turn_prob(0, 0)
                    if not second:
                        weigh(hd - 1, (g - 1) % 2, v_nat, hd - 1, v=hd - 1)
                    product(c + 2, (s + 2) % 4, xs, hooks={8: turns} if second else None)
                    if second:
                        weigh(0, 0, v_nat, 0, v=0)
                    dilated_scores(hd, g % 2)

            dilated(0, True)
            with pe.Fori(1, HEADS // 4) as i:
                dilated(i, False)

            def last_dilated_turns():
                turn_value(HEADS - 1, HEADS - 1)
                turn_prob(HEADS - 1, 1)

            out_section(C_OUT1, 80, 1, hooks={
                10: last_dilated_turns, 24: lambda: weigh(HEADS - 1, 1, v_nat, HEADS - 1, v=HEADS - 1)})
            stat_post(2, 5)
            mlp_section(C_MLP1, 96, 3, 6)

            with pe.Fori(0, LAYERS) as l:
                c0, u0, o0, v0, r0 = C_LAYER2 + N_LAYER2 * l, 16 + 28 * l, 16 + 16 * l, 16 + 9 * l, 8 + 8 * l
                rot0 = 32 + 22 * l
                stat_post(3 + l, r0 - 1)

                def diff_scores(hd):
                    def ready():
                        pe.wait_ge(sem("rotated"), rot0 + 2 * hd + 2)
                    for j in range(2):
                        a = j * (P // 2)
                        scores(u0 + 2 * hd + j, j, [(q_t[a:a + P // 2, :], k_t[a:a + P // 2, :])], ready)

                def diff_stat(hd):
                    pe.wait_ge(sem("head_squared"), DA_HEADS * l + hd + 1)
                    pe.wait_ge(sem("scale_ready"), 5 + 7 * l + hd)
                    sum_over_features([head_sq], "stat_done")

                def diff_turns(hd):
                    turn_value(v0 + hd, o0 + hd)
                    turn_prob(u0 + 2 * hd, 0, count=2)

                def diff_weigh(hd):
                    weigh(u0 + 2 * hd, 0, v_nat, o0 + hd, v=v0 + hd, count=2)

                def differential(hd):
                    c = c0 + 4 * hd
                    product(c, 0, xs)
                    diff_turns(hd - 1)
                    product(c + 1, 1, xs)
                    diff_weigh(hd - 1)
                    product(c + 2, 2, xs)
                    diff_scores(hd)
                    diff_stat(hd - 1)
                    product(c + 3, 3, xs)
                    spread(r0 + hd)

                product_first(c0, 4 + l)
                product(c0 + 3, 3, xs, hooks={STAT_AT: lambda: stat_pre(4 + l, 4 + 7 * l), SPREAD_AT: lambda: spread(r0)})
                product(c0 + 4, 0, xs, hooks={8: lambda: diff_scores(0)})
                product(c0 + 5, 1, xs, hooks={12: lambda: diff_turns(0)})
                product(c0 + 6, 2, xs)
                diff_weigh(0)
                diff_scores(1)
                diff_stat(0)
                product(c0 + 7, 3, xs)
                spread(r0 + 1)
                with pe.Fori(2, DA_HEADS) as hd:
                    differential(hd)

                c, hd = c0 + N_DA, DA_HEADS - 1
                product(c, 0, xs)
                diff_turns(hd)
                product(c + 1, 1, xs)
                diff_weigh(hd)
                product(c + 2, 2, xs)
                diff_stat(hd)
                pe.wait_ge(sem("head_squared"), DA_HEADS * l + DA_HEADS)
                turn_value(v0 + DA_HEADS, o0 + hd)
                product(c + 3, 3, xs, units=1)

                def window_turns(b):
                    for j in range(2):
                        turn_prob(u0 + 8 + 2 * b + j, j)

                def window_weigh(b):
                    for j in range(2):
                        a = j * (P // 2)
                        weigh(u0 + 8 + 2 * b + j, j, vw_nat, o0 + DA_HEADS + b, part=(a, a + P // 2))

                def window(i, first):
                    for g in range(2):
                        b, c = 2 * i + g, c0 + N_DA + N_KV + 4 * i + 2 * g
                        lone = first and g == 0
                        product(c, 2 * g, xs, hooks={15: lambda: spread(r0 + DA_HEADS)} if lone else None)
                        product(c + 1, 2 * g + 1, xs, hooks=None if lone else {14: lambda: window_turns(b - 1)})
                        if not lone:
                            window_weigh(b - 1)

                        def ready():
                            pe.wait_ge(sem("rotated"), rot0 + 11 + b)
                        for j in range(2):
                            a = j * (P // 2)
                            scores(u0 + 8 + 2 * b + j, j, [(q_t[a:a + P // 2, :], kw_t[a:a + P // 2, :])], ready)

                window(0, True)
                with pe.Fori(1, SW_BLOCKS // 2) as i:
                    window(i, False)

                def latent_stat(i):
                    pe.wait_ge(sem("latent_squared"), 2 * LATENT * l + i + 1)
                    pe.wait_ge(sem("scale_ready"), 9 + 7 * l + i // LATENT)
                    for n in range(TB):
                        mm = nc.tensor.matmul(extra[:, TOKENS + n:TOKENS + n + 1], latent_sq[:, i % 2, n * P:(n + 1) * P],
                                              ones[:, 0:1], start=(i % LATENT == 0 and n == 0),
                                              stop=(i % LATENT == LATENT - 1), skip_group_check=True)
                    mm.then_inc(sem("latent_counted"), 1)

                c = c0 + N_DA + N_KV + N_SW
                for i in range(N_LATENT):
                    hooks = {1: {14: lambda: window_turns(SW_BLOCKS - 1)}, LATENT + 2: {4: lambda: spread(r0 + 5)}}
                    product(c + i, i % 4, xs, hooks=hooks.get(i))
                    if i == 1:
                        window_weigh(SW_BLOCKS - 1)
                    if 1 <= i <= LATENT:
                        latent_stat(i - 1)
                    if i > LATENT + 1:
                        latent_stat(i - 2)

                def latent_products(c, s, hd):
                    s2 = (s + 2) % 4
                    where = [acc[s][:, 0:TOKENS], acc[s][:, TOKENS:], acc[s2][:, 0:TOKENS], acc[s2][:, TOKENS:]]
                    base = [0, LATENT, LATENT, 0]
                    pe.wait_ge(high_ready, c + 1)
                    pe.wait_ge(summed, c - 1 + int(hd == 0))
                    pe.wait_ge(sem("latent_ready"), 2 * LATENT * (l + 1))
                    for m in range(4):
                        for kt in range(LATENT):
                            w = w_high[:, s, (LATENT * m + kt) * P:(LATENT * m + kt + 1) * P]
                            for part in range(2):
                                nc.tensor.matmul(where[m], w, latent[:, base[m] + kt, part, :],
                                                 start=(m % 2 == 0 and kt == 0 and part == 0), stop=False,
                                                 skip_group_check=True)
                    pe.wait_ge(low_ready, c + 1)
                    for m in range(4):
                        for kt in range(LATENT):
                            w = w_low[:, s, (LATENT * m + kt) * P:(LATENT * m + kt + 1) * P]
                            mm = nc.tensor.matmul(where[m], w, latent[:, base[m] + kt, 0, :], start=False,
                                                  stop=(kt == LATENT - 1), skip_group_check=True)
                    mm.then_inc(product_done, 1)

                def mla_turns(hd):
                    turn_value(v0 + 5 + hd, o0 + 12 + hd)
                    turn_prob(u0 + 24 + hd, hd % 2)

                def mla_weigh(hd):
                    weigh(u0 + 24 + hd, hd % 2, v_nat, o0 + 12 + hd, v=v0 + 5 + hd)

                def mla_scores(hd):
                    a = (hd % 2) * (P // 2)

                    def ready():
                        pe.wait_ge(sem("rotated"), rot0 + 19 + hd)
                        pe.wait_ge(sem("nope_ready"), MLA_HEADS * l + hd + 1)
                    scores(u0 + 24 + hd, hd % 2, [(q_t, k_t), (qr_t[a:a + P // 2, :], kr_t[a:a + P // 2, :])], ready)

                c = c + N_LATENT
                for hd in range(MLA_HEADS):
                    hooks = {6: lambda: mla_scores(hd - 1)} if hd else {
                        4: lambda: latent_stat(N_LATENT - 2), 12: lambda: latent_stat(N_LATENT - 1)}
                    if hd > 1:
                        hooks[2] = lambda: mla_weigh(hd - 2)
                    product(c + 2 * hd, (2 * hd) % 4, xs, hooks=hooks)
                    if hd == 0:
                        spread(r0 + 6)
                    latent_products(c + 2 * hd + 1, (2 * hd + 1) % 4, hd)
                    if hd:
                        mla_turns(hd - 1)
                hd = MLA_HEADS - 1
                out_section(c + N_MLA, 160 + KB * l, 2, hooks={
                    2: lambda: mla_weigh(hd - 1), 6: lambda: mla_scores(hd), 34: lambda: mla_turns(hd),
                    41: lambda: mla_weigh(hd)})
            stat_post(NORMS - 1, 23)

        @block.scalar
        def _(act):
            def high(c, s, units=UNITS):
                act.wait_ge(landed[s], (c - s) * 4 + 16)
                nc.scalar.activation(w_high[:, s, 0:units * P], raw[:, s, 0:units * P], ACT.Copy)\
                    .then_inc(high_ready, 1)

            def ahead(c, s, units=UNITS):
                high(c + AHEAD, (s + AHEAD) % 4, units)

            def corr_out(c, s):
                act.wait_ge(product_done, c + 1)
                act.wait_ge(summed, at(c - 1))
                nc.scalar.activation(corr[:, s % 2, :], acc[s][:, TOKENS:], ACT.Copy).then_inc(corr_ready, 1)

            def square(src, k, s, ready):
                ready()
                act.wait_ge(sem("square_added"), at(k - 1))
                nc.scalar.activation(sq[:, s % 2, :], src, ACT.Square).then_inc(sem("squared"), 1)

            def input_high(n, b):
                nc.scalar.activation(xs[:, b, 0, :], h[:, b, :], ACT.Copy,
                                     scale=column(G_PRE + KB * n + b)).then_inc(sem("xs_high"), 1)

            def norm_input(n, c):
                for b in range(KB):
                    act.wait_ge(sem("h_ready"), KB * (n - 1) + b + 1)
                    input_high(n, b)
                    square(h[:, b, :], squares_pre(n) + b, b, lambda: None)
                    if b == KB // 2:
                        high(c + 3, 3)

            def gain(m, b):
                act.wait_ge(sem("squared"), squares_post(m) + b + 1)
                nc.scalar.activation(dyn(branch, b), dyn(branch, b), ACT.Copy, scale=column(G_POST + KB * m + b))\
                    .then_inc(sem("gained"), 1)

            def out_section(c0, m):
                def four(i):
                    for s in range(4):
                        c = c0 + 4 * i + s
                        corr_out(c, s)
                        if s < 3:
                            ahead(c, s)
                        square(dyn(branch, 4 * i + s), squares_post(m) + 4 * i + s, s,
                               lambda: act.wait_ge(summed, c + 1))
                        if s == 3:
                            ahead(c, s)
                        gain(m, 4 * i + s)
                with act.Fori(0, KB // 4) as i:
                    four(i)

            def split_high(src, b, s):
                act.wait_ge(sem("source_ready"), src + 1)
                nc.scalar.activation(dyn2(inner, b, 0), source[:, s, :], ACT.Copy).then_inc(sem("inner_high"), 1)

            def mlp_section(c0, src0, m):
                def quarter(q, first, last):
                    def up_four(i, first_four):
                        for s in range(4):
                            j = 4 * i + s
                            c = c0 + 2 * KB * q + j
                            corr_out(c, s)
                            if not (first_four and s == 0):
                                ahead(c, s)
                            split_high(src0 + KB * q + j, j, s % 2)
                    if first:
                        up_four(0, True)
                    with act.Fori(int(first), KB // 4) as i:
                        up_four(i, False)
                    with act.Fori(0, KB // 4) as i:
                        for s in range(4):
                            b = 4 * i + s
                            c = c0 + 2 * KB * q + KB + b
                            corr_out(c, s)
                            if s < 3 or not last:
                                ahead(c, s)
                            if last:
                                square(dyn(branch, b), squares_post(m) + b, s,
                                       lambda: act.wait_ge(sem("down_added"), 3 * KB * (m // 2) + 2 * KB + b + 1))
                                if s == 3:
                                    ahead(c, s)
                                gain(m, b)
                quarter(0, True, False)
                with act.Fori(1, FFN_QUARTERS - 1) as q:
                    quarter(q, False, False)
                quarter(FFN_QUARTERS - 1, False, True)

            def swap(rot, c, s, half):
                act.wait_ge(summed, c + 1)
                act.wait_ge(sem("rot_sin"), at(rot))
                exchange(y[:, s % 2, :], half)

            def exchange(src, half):
                for a in range(0, P, half):
                    b = a + half if (a // half) % 2 == 0 else a - half
                    cp = nc.scalar.activation(swapped[a:a + half, :], src[b:b + half, :], ACT.Copy)
                cp.then_inc(sem("swapped_ready"), 1)

            def exp_scores(u, bank, sink=None):
                act.wait_ge(sem("negmax_ready"), u + 1)
                for t, (lo, hi) in enumerate(((0, P), (P, COLS))):
                    nc.scalar.activation(prob[:, bank, lo:hi], prob[:, bank, lo:hi], ACT.Exp,
                                         bias=neg_max(bank, t), accum_out=denom(bank, t)).then_inc(sem("exp_ready"), 1)
                if sink is not None:
                    nc.scalar.activation(exp_sink(bank), neg_max(bank), ACT.Exp, bias=sink)\
                        .then_inc(sem("sink_ready"), 1)

            def copy_prob(u, bank, count=1):
                act.wait_ge(sem("prob_turned"), u + count)
                nc.scalar.activation(prob_t[:, bank, :], score[bank][:, 0:COLS], ACT.Copy)\
                    .then_inc(sem("prob_t_ready"), count)

            def copy_value(v, to):
                act.wait_ge(sem("v_turned"), v + 1)
                nc.scalar.activation(to[:, :, :], head_out[:, TOKENS:].rearrange("p (n f) -> p n f", n=TB), ACT.Copy)\
                    .then_inc(sem("v_ready"), 1)

            act.wait_ge(sem("columns_landed"), 16)
            for b in range(KB):
                if b % 4 == 0:
                    act.wait_ge(sem(f"x_landed_{b // 4}"), 16)
                if b in FIRST_SPLITS:
                    high(FIRST_SPLITS.index(b), FIRST_SPLITS.index(b))
                input_high(0, b)
            high(2, 2)
            for b in range(KB):
                square(h[:, b, :], b, b, lambda: None)
            def copy_av(j):
                act.wait_ge(sem("av_turned"), j + 1)
                nc.scalar.activation(a_v[:, :, j * P:(j + 1) * P],
                                     head_out[:, 0:TOKENS].rearrange("p (n f) -> p n f", n=TB), ACT.Copy)\
                    .then_inc(sem("av_copied"), 1)

            for j in range(A_BLOCKS):
                corr_out(j, j % 4)
                ahead(j, j % 4)
                act.wait_ge(sem("av_scaled"), j + 1)
                act.wait_ge(sem("av_turned"), at(j - 1))
                nc.scalar.activation((q_t, k_t)[j % 2][:, :], scaled[:, j % 2, :], ACT.Gelu_apprx_tanh)\
                    .then_inc(sem("av_gelu"), 1)
                if j:
                    copy_av(j - 1)

            def gating(j, first):
                c = A_BLOCKS + 4 * j
                for s in range(4):
                    corr_out(c + s, s)
                    if first and s == 0:
                        copy_av(A_BLOCKS - 1)
                    if s == 3:
                        act.wait_ge(sem("au_scaled"), j + 1)
                        act.wait_ge(sem("source_ready"), at(2 * j))
                        nc.scalar.activation(k_t[:, :], scaled[:, 1, :], ACT.Gelu_apprx_tanh)\
                            .then_inc(sem("au_gelu"), 1)
                    ahead(c + s, s)
                    if s == 2:
                        split_high(2 * j, A_BLOCKS + j, 0)
                    if s == 3:
                        split_high(2 * j + 1, j, 1)

            gating(0, True)
            with act.Fori(1, A_BLOCKS) as j:
                gating(j, False)
            out_section(C_OUT0, 0)
            norm_input(1, C_MLP0)
            for i in range(2):
                act.wait_ge(sem("angle_ready"), i + 1)
                nc.scalar.activation(rope2[:, i, :], rope2[:, i, :], ACT.Sin).then_inc(sem("sine_ready"), 1)
            act.wait_ge(sem("dots_ready"), 1)
            nc.scalar.activation(lam_exp, lam_dot, ACT.Exp).then_inc(sem("lam_exp_ready"), 1)
            mlp_section(C_MLP0, 16, 1)
            norm_input(2, C_QKV)

            def head_high(hd):
                act.wait_ge(sem("head_done"), hd + 1)
                nc.scalar.activation(dyn2(inner, hd, 0), head_out[:, 0:TOKENS], ACT.Copy)\
                    .then_inc(sem("inner_high"), 1)

            def dilated(i, first):
                for g in range(4):
                    hd, c = 4 * i + g, C_QKV + 12 * i + 3 * g
                    s = (3 * g) % 4
                    lone = first and g == 0
                    corr_out(c, s)
                    if not lone:
                        ahead(c, s)
                    swap(2 * hd, c, s, P // 2)
                    if not lone:
                        copy_value(hd - 1, v_nat)
                        copy_prob(hd - 1, (g - 1) % 2)
                    corr_out(c + 1, (s + 1) % 4)
                    ahead(c + 1, (s + 1) % 4)
                    swap(2 * hd + 1, c + 1, (s + 1) % 4, P // 2)
                    if not lone:
                        head_high(hd - 1)
                    corr_out(c + 2, (s + 2) % 4)
                    ahead(c + 2, (s + 2) % 4)
                    exp_scores(hd, g % 2)

            dilated(0, True)
            with act.Fori(1, HEADS // 4) as i:
                dilated(i, False)
            copy_value(HEADS - 1, v_nat)
            copy_prob(HEADS - 1, 1)
            head_high(HEADS - 1)
            out_section(C_OUT1, 2)
            norm_input(3, C_MLP1)
            mlp_section(C_MLP1, 80, 3)

            with act.Fori(0, LAYERS) as l:
                c0, u0, o0, v0 = C_LAYER2 + N_LAYER2 * l, 16 + 28 * l, 16 + 16 * l, 16 + 9 * l
                rot0, gate0, src0, done0 = 32 + 22 * l, 16 * l, 144 + 16 * l, 16 + 24 * l
                norm_input(4 + l, c0)

                def gate_tanh(g):
                    act.wait_ge(sem("gate_scaled"), gate0 + g + 1)
                    nc.scalar.activation(tanh_g[:, :], scaled[:, 1, :], ACT.Tanh, scale=0.5)\
                        .then_inc(sem("tanh_ready"), 1)

                def diff_square(hd):
                    act.wait_ge(sem("head_done"), done0 + hd + 1)
                    nc.scalar.activation(head_sq[:, :], head_out[:, 0:TOKENS], ACT.Square)\
                        .then_inc(sem("head_squared"), 1)

                def differential(hd, first):
                    c = c0 + 4 * hd
                    corr_out(c, 0)
                    if not first:
                        ahead(c, 0)
                    swap(rot0 + 2 * hd, c, 0, 32)
                    if not first:
                        copy_value(v0 + hd - 1, v_nat)
                        copy_prob(u0 + 2 * hd - 2, 0, count=2)
                    corr_out(c + 1, 1)
                    ahead(c + 1, 1)
                    swap(rot0 + 2 * hd + 1, c + 1, 1, 32)
                    if not first:
                        diff_square(hd - 1)
                    corr_out(c + 2, 2)
                    ahead(c + 2, 2)
                    for j in range(2):
                        exp_scores(u0 + 2 * hd + j, j)
                    corr_out(c + 3, 3)
                    ahead(c + 3, 3)
                    gate_tanh(hd)
                    if not first:
                        split_high(src0 + hd - 1, hd - 1, 0)

                differential(0, True)
                with act.Fori(1, DA_HEADS) as hd:
                    differential(hd, False)

                c, hd = c0 + N_DA, DA_HEADS - 1
                corr_out(c, 0)
                ahead(c, 0, units=1)
                swap(rot0 + 8, c, 0, 32)
                copy_value(v0 + hd, v_nat)
                copy_prob(u0 + 2 * hd, 0, count=2)
                corr_out(c + 1, 1)
                ahead(c + 1, 1)
                diff_square(hd)
                corr_out(c + 2, 2)
                ahead(c + 2, 2)
                swap(rot0 + 9, c + 2, 2, 32)
                copy_value(v0 + DA_HEADS, vw_nat)
                corr_out(c + 3, 3)
                ahead(c + 3, 3)
                split_high(src0 + hd, hd, 0)

                def window_copies(b):
                    for j in range(2):
                        copy_prob(u0 + 8 + 2 * b + j, j)

                def window(i, first):
                    for g in range(2):
                        b, c = 2 * i + g, c0 + N_DA + N_KV + 4 * i + 2 * g
                        lone = first and g == 0
                        corr_out(c, 2 * g)
                        ahead(c, 2 * g)
                        swap(rot0 + 10 + b, c, 2 * g, 32)
                        if not lone:
                            window_copies(b - 1)
                        corr_out(c + 1, 2 * g + 1)
                        ahead(c + 1, 2 * g + 1)
                        gate_tanh(DA_HEADS + b)
                        for j in range(2):
                            exp_scores(u0 + 8 + 2 * b + j, j, sink=column(SINK + 16 * l + 8 * j + b))
                        if not lone:
                            split_high(src0 + DA_HEADS + b - 1, DA_HEADS + b - 1, 0)

                window(0, True)
                with act.Fori(1, SW_BLOCKS // 2) as i:
                    window(i, False)

                c = c0 + N_DA + N_KV + N_SW
                for i in range(N_LATENT):
                    if i == 1:
                        window_copies(SW_BLOCKS - 1)
                    corr_out(c + i, i % 4)
                    ahead(c + i, i % 4)
                    act.wait_ge(sem("latent_scaled"), N_LATENT * l + i + 1)
                    nc.scalar.activation(latent[:, i, 0, :], scaled[:, i % 2, :], ACT.Copy,
                                         scale=latent_gain(l, i)).then_inc(sem("latent_high"), 1)
                    if i > 1:
                        act.wait_ge(sem("latent_counted"), N_LATENT * l + i - 1)
                    nc.scalar.activation(latent_sq[:, i % 2, :], scaled[:, i % 2, :], ACT.Square)\
                        .then_inc(sem("latent_squared"), 1)
                    if i == 1:
                        split_high(src0 + 11, 11, 0)

                c = c + N_LATENT
                for hd in range(MLA_HEADS):
                    s = (2 * hd) % 4
                    if hd > 1:
                        split_high(src0 + 10 + hd, 10 + hd, 0)
                    if hd:
                        exp_scores(u0 + 23 + hd, (hd - 1) % 2)
                    corr_out(c + 2 * hd, s)
                    ahead(c + 2 * hd, s)
                    gate_tanh(12 + hd)
                    corr_out(c + 2 * hd + 1, (s + 3) % 4)
                    act.wait_ge(sem("rot_sin"), rot0 + 18 + hd)
                    exchange(acc[(s + 3) % 4][:, TOKENS:], 32)
                    if hd:
                        copy_value(v0 + 4 + hd, v_nat)
                        copy_prob(u0 + 23 + hd, (hd - 1) % 2)
                    ahead(c + 2 * hd + 1, s + 1)
                split_high(src0 + 14, 14, 0)
                exp_scores(u0 + 27, 1)
                copy_value(v0 + 8, v_nat)
                copy_prob(u0 + 27, 1)
                split_high(src0 + 15, 15, 0)
                out_section(c + N_MLA, 4 + l)

        @block.gpsimd
        def _(pool):
            def add_squares(k0, stats=None, count=KB):
                pool.wait_ge(sem("squared"), k0 + 2)
                pool.wait_ge(sem("square_added"), k0)
                if stats is not None:
                    pool.wait_ge(sem("stat_done"), stats)
                nc.gpsimd.tensor_tensor(sum_sq[:, :], sq[:, 0, :], sq[:, 1, :], ALU.add)\
                    .then_inc(sem("square_added"), 2)
                for b in range(2, count):
                    pool.wait_ge(sem("squared"), k0 + b + 1)
                    pool.wait_ge(sem("square_added"), k0 + b)
                    nc.gpsimd.tensor_tensor(sum_sq[:, :], sum_sq[:, :], sq[:, b % 2, :], ALU.add)\
                        .then_inc(sem("square_added"), 1)

            def root(r):
                pool.wait_ge(sem("mean_ready"), r + 1)
                nc.gpsimd.tensor_tensor(root_of, mean_of, minus_half[:, :], ALU.pow).then_inc(sem("root_ready"), 1)

            nc.gpsimd.memset(minus_half[:, :], -0.5).then_inc(sem("half_set"), 1)
            nc.gpsimd.memset(conv_in[:, 0:2], 0.0).then_inc(sem("pad_set"), 1)
            pool.wait_ge(sem("half_set"), 1)
            add_squares(squares_pre(0))
            root(0)
            pool.wait_ge(sem("spatial_landed"), 16)
            nc.gpsimd.affine_select(out=spatial, in_=spatial, compare_op=ALU.is_ge, fill=0.0, base=0,
                                    pattern=[[0, A_BLOCKS], [1, P]], channel_multiplier=-1)\
                .then_inc(sem("spatial_ready"), 1)
            pool.wait_ge(sem("av_var_ready"), 1)
            nc.gpsimd.tensor_tensor(av_root, av_var, minus_half[:, :], ALU.pow).then_inc(sem("av_root_ready"), 1)
            for m in range(3):
                add_squares(squares_post(m), m + 1, KB - 1)
                root(2 * m + 1)
                add_squares(squares_pre(m + 1))
                root(2 * m + 2)
            with pool.Fori(0, LAYERS) as l:
                add_squares(squares_post(3 + l), 4 + 5 * l, KB - 1)
                root(7 + 8 * l)
                add_squares(squares_pre(4 + l))
                for i in range(7):
                    root(8 + 8 * l + i)
            add_squares(squares_post(NORMS - 1), 14, KB - 1)
            root(23)

        @block.vector
        def _(dve):
            V = nc.vector

            def low(c, s, units=UNITS):
                dve.wait_ge(high_ready, c + 1)
                V.tensor_tensor(w_low[:, s, 0:units * P], raw[:, s, 0:units * P], w_high[:, s, 0:units * P],
                                ALU.subtract).then_inc(low_ready, 1)

            def ahead(c, s, units=UNITS):
                low(c + AHEAD, (s + AHEAD) % 4, units)

            def sum_halves(c, s, to=None):
                dve.wait_ge(corr_ready, c + 1)
                V.tensor_tensor(y[:, s % 2, :] if to is None else to, acc[s][:, 0:TOKENS], corr[:, s % 2, :], ALU.add)\
                    .then_inc(summed, 1)

            def scale_by(to, c, s, scale, done):
                dve.wait_ge(summed, c + 1)
                V.tensor_tensor(to, y[:, s % 2, :], scale, ALU.mult).then_inc(sem(done), 1)

            def mean(r, count, eps, stat_sem, value):
                dve.wait_ge(sem(stat_sem), value)
                V.tensor_scalar(mean_of, extra[:, TOKENS:TOKENS + TB], 1.0 / count, eps, ALU.mult, ALU.add)\
                    .then_inc(sem("mean_ready"), 1)
                dve.wait_ge(sem("root_ready"), r + 1)
                for n in range(TB):
                    op = V.tensor_scalar(diag[:, n * P:(n + 1) * P], ident, root_of[:, n:n + 1], None, ALU.mult)
                op.then_inc(sem("diag_ready"), 1)

            def scale_out(r, copied, to):
                dve.wait_ge(sem("spread_done"), r + 1)
                V.tensor_copy(to, extra[:, 0:TOKENS]).then_inc(sem("scale_ready"), 1)
                dve.wait_ge(sem("scale_ready"), copied + 1)

            def xs_low(n, b):
                dve.wait_ge(sem("xs_high"), KB * n + b + 1)
                V.scalar_tensor_tensor(out=xs[:, b, 1, :], in0=h[:, b, :], scalar=column(G_PRE + KB * n + b),
                                       in1=xs[:, b, 0, :], op0=ALU.mult, op1=ALU.subtract)\
                    .then_inc(sem("xs_ready"), 1)

            def norm(m, n, r, c):
                mean(r, D, NORM_EPS, "square_added", squares_post(m) + KB)
                if c is not None:
                    low(c + 2, 2)
                dve.wait_ge(sem("spread_done"), r + 1)
                late = []
                for b, width in NORM_GROUPS:
                    scale = extra[:, 0:TOKENS].unsqueeze(1).to_broadcast([P, width, TOKENS])
                    dve.wait_ge(sem("gained"), KB * m + b + width)
                    dve.wait_ge(sem("h_ready"), at(KB * m + b))
                    V.tensor_tensor(step[:, 0:width, :], branch[:, b:b + width, :], scale, ALU.mult)\
                        .then_inc(sem("step_ready"), width)
                    if late:
                        xs_low(n, late.pop(0))
                    dve.wait_ge(sem("step_ready"), KB * m + b + width)
                    V.tensor_tensor(h[:, b:b + width, :], h[:, b:b + width, :], step[:, 0:width, :], ALU.add)\
                        .then_inc(sem("h_ready"), width)
                    for i in late:
                        xs_low(n, i)
                    late = list(range(b, b + width)) if c is not None else []
                for i in late:
                    xs_low(n, i)
                if c is not None:
                    low(c + 3, 3)

            def norm_scale(r, sd, copied):
                mean(r, D, NORM_EPS, "stat_done", sd + 1)
                scale_out(r, copied, scale_pre[:, :])

            def split_low(split, b, s):
                dve.wait_ge(sem("inner_high"), split + 1)
                V.tensor_tensor(dyn2(inner, b, 1), source[:, s, :], dyn2(inner, b, 0), ALU.subtract)\
                    .then_inc(sem("inner_ready"), 1)

            def out_section(c0):
                def four(i, last):
                    for s in range(4):
                        c = c0 + 4 * i + s
                        sum_halves(c, s, dyn(branch, 4 * i + s))
                        if s < 3 or not last:
                            ahead(c, s)
                with dve.Fori(0, KB // 4 - 1) as i:
                    four(i, False)
                four(KB // 4 - 1, True)

            def mlp_section(c0, split0, up0):
                def quarter(q, first, last):
                    def up_four(i, first_four):
                        for s in range(4):
                            j = 4 * i + s
                            c = c0 + 2 * KB * q + j
                            up = up0 + KB * q + j
                            sum_halves(c, s)
                            scale_by(scaled[:, s % 2, :], c, s, scale_pre[:, :], "up_scaled")
                            dve.wait_ge(sem("up_scaled"), up + 1)
                            V.scalar_tensor_tensor(out=source[:, s % 2, :], in0=scaled[:, s % 2, :], scalar=0.0,
                                                   in1=scaled[:, s % 2, :], op0=ALU.max, op1=ALU.mult)\
                                .then_inc(sem("source_ready"), 1)
                            if not (first_four and s == 0):
                                ahead(c, s)
                            split_low(split0 + KB * q + j, j, s % 2)

                    if first:
                        up_four(0, True)
                    with dve.Fori(int(first), KB // 4) as i:
                        up_four(i, False)

                    def four(i, last_four):
                        for s in range(4):
                            b = 4 * i + s
                            c = c0 + 2 * KB * q + KB + b
                            if first:
                                sum_halves(c, s, dyn(branch, b))
                            else:
                                sum_halves(c, s)
                                dve.wait_ge(summed, c + 1)
                                V.tensor_tensor(dyn(branch, b), dyn(branch, b), y[:, s % 2, :], ALU.add)\
                                    .then_inc(sem("down_added"), 1)
                            if not (last_four and s == 3):
                                ahead(c, s)
                    with dve.Fori(0, KB // 4 - int(last)) as i:
                        four(i, False)
                    if last:
                        four(KB // 4 - 1, True)
                quarter(0, True, False)
                with dve.Fori(1, FFN_QUARTERS - 1) as q:
                    quarter(q, False, False)
                quarter(FFN_QUARTERS - 1, False, True)

            def rotate_cos(c, s, table):
                dve.wait_ge(summed, c + 1)
                V.tensor_tensor(scaled[:, 0, :], y[:, s % 2, :], table[:, 0, :], ALU.mult).then_inc(sem("rot_cos"), 1)

            def rotate(rot, cos, table, to, free):
                dve.wait_ge(sem("swapped_ready"), rot + 1)
                V.tensor_tensor(turned[:, :], swapped[:, :], table[:, 1, :], ALU.mult).then_inc(sem("rot_sin"), 1)
                dve.wait_ge(sem("rot_sin"), rot + 1)
                dve.wait_ge(sem("rot_cos"), cos + 1)
                free()
                V.tensor_tensor(to[:, :], scaled[:, 0, :], turned[:, :], ALU.add).then_inc(sem("rotated"), 1)

            def mask_max(u, bank, mask, scale, neg_sink=None):
                dve.wait_ge(sem("scores_done"), u + 1)
                dve.wait_ge(sem("prob_turned"), at(u - 1))
                V.scalar_tensor_tensor(out=prob[:, bank, :], in0=score[bank][:, 0:COLS], scalar=scale, in1=mask,
                                       op0=ALU.mult, op1=ALU.add).then_inc(sem("masked"), 1)
                dve.wait_ge(sem("masked"), u + 1)
                for t, (lo, hi) in enumerate(((0, P), (P, COLS))):
                    op = V.tensor_reduce(neg_max(bank, t), prob[:, bank, lo:hi], AXIS_X, ALU.max, negate=True)
                if neg_sink is not None:
                    op.then_inc(sem("window_maxed"), 1)
                    dve.wait_ge(sem("window_maxed"), neg_sink[1] + 1)
                    op = V.tensor_scalar(neg_max(bank), neg_max(bank), neg_sink[0], None, ALU.min)
                op.then_inc(sem("negmax_ready"), 1)

            def normalise(u, bank, sink=None):
                dve.wait_ge(sem("exp_ready"), 2 * u + 2)
                if sink is not None:
                    dve.wait_ge(sem("sink_ready"), sink + 1)
                    V.tensor_tensor(denom(bank), denom(bank), exp_sink(bank), ALU.add).then_inc(sem("sink_added"), 1)
                    dve.wait_ge(sem("sink_added"), sink + 1)
                V.reciprocal(inverse(bank), denom(bank)).then_inc(sem("inverse_ready"), 1)
                dve.wait_ge(sem("inverse_ready"), u + 1)
                for t, (lo, hi) in enumerate(((0, P), (P, COLS))):
                    op = V.tensor_scalar(prob[:, bank, lo:hi], prob[:, bank, lo:hi], inverse(bank, t), None, ALU.mult)
                op.then_inc(sem("prob_ready"), 1)

            dve.wait_ge(sem("columns_landed"), 16)
            for b in range(KB):
                if b in FIRST_SPLITS:
                    low(FIRST_SPLITS.index(b), FIRST_SPLITS.index(b))
                xs_low(0, b)
            low(2, 2)
            norm_scale(0, 0, 0)

            for j in range(A_BLOCKS):
                sum_halves(j, j % 4)
                dve.wait_ge(sem("av_gelu"), at(j - 1))
                scale_by(scaled[:, j % 2, :], j, j, scale_pre[:, :], "av_scaled")
                ahead(j, j % 4)

            def gating(j, first):
                c = A_BLOCKS + 4 * j
                sum_halves(c, 0)
                scale_by(v_t[:, :], c, 0, scale_pre[:, :], "gc_ready")
                ahead(c, 0)
                if first:
                    dve.wait_ge(sem("av_copied"), A_BLOCKS)
                    for n in range(TB):
                        for k in range(2):
                            V.bn_stats(bn[:, n, k, :], a_v[:, n, k * 512:(k + 1) * 512]).then_inc(sem("av_stats"), 1)
                    dve.wait_ge(sem("av_stats"), 4)
                    for n in range(TB):
                        V.bn_aggr(av_moments[:, 2 * n:2 * n + 2], bn[:, n, :, :]).then_inc(sem("av_moments"), 1)
                    dve.wait_ge(sem("av_moments"), 2)
                    V.tensor_scalar(av_var, av_moments[:, 1:4:2], LN_EPS, None, ALU.add).then_inc(sem("av_var_ready"), 1)
                    dve.wait_ge(sem("av_root_ready"), 1)
                    dve.wait_ge(sem("bias_landed"), 16)
                    dve.wait_ge(sem("pad_set"), 1)
                sum_halves(c + 1, 1)
                scale_by(scaled[:, 1, :], c + 1, 1, scale_pre[:, :], "bx_scaled")
                dve.wait_ge(sem("bx_scaled"), j + 1)
                dve.wait_ge(sem("gc_ready"), j + 1)
                V.tensor_tensor(conv_in[:, 2:], scaled[:, 1, :], v_t[:, :], ALU.mult).then_inc(sem("conv_in_ready"), 1)
                dve.wait_ge(sem("conv_in_ready"), j + 1)
                V.tensor_scalar(q_t[:, :], conv_in[:, 0:TOKENS], column(CONV + j), None, ALU.mult)\
                    .then_inc(sem("tap"), 1)
                for tap in (1, 2):
                    dve.wait_ge(sem("tap"), 3 * j + tap)
                    V.scalar_tensor_tensor(out=q_t[:, :], in0=conv_in[:, tap:tap + TOKENS],
                                           scalar=column(CONV + A_BLOCKS * tap + j), in1=q_t[:, :],
                                           op0=ALU.mult, op1=ALU.add).then_inc(sem("tap"), 1)
                ahead(c + 1, 1)
                dve.wait_ge(sem("mix_done"), at(j))
                for n in range(TB):
                    src = a_v[:, n, :].rearrange("p (j f) -> p j f", f=P)
                    op = V.tensor_scalar(v_nat[:, n, :], dyn(src, j), av_moments[:, 2 * n:2 * n + 1],
                                         av_root[:, n:n + 1], ALU.subtract, ALU.mult)
                op.then_inc(sem("av_staged"), 1)
                sum_halves(c + 2, 2)
                scale_by(scaled[:, 0, :], c + 2, 2, scale_pre[:, :], "gb_scaled")
                dve.wait_ge(sem("gb_scaled"), j + 1)
                dve.wait_ge(sem("tap"), 3 * j + 3)
                V.tensor_tensor(source[:, 0, :], scaled[:, 0, :], q_t[:, :], ALU.mult).then_inc(sem("source_ready"), 1)
                ahead(c + 2, 2)
                split_low(2 * j, A_BLOCKS + j, 0)
                sum_halves(c + 3, 3)
                scale_by(scaled[:, 1, :], c + 3, 3, scale_pre[:, :], "au_scaled")
                dve.wait_ge(sem("mix_done"), j + 1)
                for n in range(TB):
                    op = V.tensor_tensor(turned[:, n * P:(n + 1) * P], head_out[:, n * P:(n + 1) * P], dyn(bias_s, j),
                                         ALU.add)
                op.then_inc(sem("mix_read"), 1)
                dve.wait_ge(sem("mix_read"), j + 1)
                dve.wait_ge(sem("au_gelu"), j + 1)
                V.tensor_tensor(source[:, 1, :], k_t[:, :], turned[:, :], ALU.mult).then_inc(sem("source_ready"), 1)
                ahead(c + 3, 3)
                split_low(2 * j + 1, j, 1)

            gating(0, True)
            with dve.Fori(1, A_BLOCKS) as j:
                gating(j, False)
            dve.wait_ge(sem("positions_landed"), 16)
            chain = [0]

            def link(op):
                chain[0] += 1
                op.then_inc(sem("setup"), 1)
                dve.wait_ge(sem("setup"), chain[0])

            round_to_int = 1.5 * 2.0 ** 23
            two_pi = 2 * math.pi
            pi_high = 6.28125
            pi_mid = float(np.float32(round((two_pi - pi_high) * 2 ** 22) / 2 ** 22))
            pi_low = float(np.float32(two_pi - pi_high - pi_mid))
            limit = float(np.nextafter(np.float32(math.pi), np.float32(0)))
            link(V.tensor_copy(kw_t[:, :], gate[:, :].bitcast(I32)))
            link(V.tensor_scalar(kw_t[:, :], kw_t[:, :], column(INV_FREQ), None, ALU.mult))
            for i, (turn, shift) in enumerate(((0.25, math.pi / 2), (0.0, 0.0))):
                link(V.tensor_scalar(kr_t[:, :], kw_t[:, :], 1.0 / two_pi, turn, ALU.mult, ALU.add))
                link(V.tensor_scalar(kr_t[:, :], kr_t[:, :], round_to_int, None, ALU.add))
                link(V.tensor_scalar(kr_t[:, :], kr_t[:, :], round_to_int, None, ALU.subtract))
                link(V.scalar_tensor_tensor(out=rope2[:, i, :], in0=kr_t[:, :], scalar=-pi_high, in1=kw_t[:, :],
                                            op0=ALU.mult, op1=ALU.add))
                for part in (-pi_mid, -pi_low):
                    link(V.scalar_tensor_tensor(out=rope2[:, i, :], in0=kr_t[:, :], scalar=part, in1=rope2[:, i, :],
                                                op0=ALU.mult, op1=ALU.add))
                link(V.tensor_scalar(rope2[:, i, :], rope2[:, i, :], shift, limit, ALU.add, ALU.min))
                V.tensor_scalar(rope2[:, i, :], rope2[:, i, :], -limit, None, ALU.max).then_inc(sem("angle_ready"), 1)
            dve.wait_ge(sem("lambdas_landed"), 16)
            pairs = lam_vectors.rearrange("p l (i a f) -> p l i a f", i=2, a=2)
            products = tanh_g[:, :].rearrange("p (l i f) -> p l i f", l=LAYERS, i=2)
            for i in range(2):
                link(V.tensor_tensor(products[:, :, i], pairs[:, :, i, 0], pairs[:, :, i, 1], ALU.mult))
            V.tensor_reduce(lam_dot, tanh_g[:, :].rearrange("p (i f) -> p i f", f=64), AXIS_X, ALU.add)\
                .then_inc(sem("dots_ready"), 1)
            V.tensor_scalar(neg_sinks, col[:, SINK:SINK + 16 * LAYERS], -1.0, None, ALU.mult).then_inc(sem("sinks_ready"), 1)
            V.tensor_tensor(subln_gain, col[:, SUBLN:SUBLN + LAYERS], col[:, LAM_INIT + LAYERS:LAM_INIT + 2 * LAYERS],
                            ALU.mult).then_inc(sem("gains_ready"), 1)

            out_section(C_OUT0)
            norm(0, 1, 1, C_MLP0)
            norm_scale(2, 1, 1)
            mlp_section(C_MLP0, 16, 0)
            norm(1, 2, 3, C_QKV)
            norm_scale(4, 2, 2)
            dve.wait_ge(sem("lam_exp_ready"), 1)
            link(V.tensor_tensor(lam, lam_exp[:, 0:2 * LAYERS:2], lam_exp[:, 1:2 * LAYERS:2], ALU.subtract))
            link(V.tensor_tensor(lam, lam, col[:, LAM_INIT:LAM_INIT + LAYERS], ALU.add))
            dve.wait_ge(sem("sine_ready"), 2)
            link(V.tensor_scalar(rope2[:, 1, :], rope2[:, 1, :], column(SIGN), None, ALU.mult))
            dve.wait_ge(sem("sinks_ready"), 1)
            dve.wait_ge(sem("gains_ready"), 1)


            def scaled_tables(table, to, scale, done, count):
                for i in range(2):
                    op = V.tensor_tensor(to[:, i, :], table[:, i, :], scale, ALU.mult)
                op.then_inc(sem(done), 1)
                dve.wait_ge(sem(done), at(count))

            scaled_tables(rope1, rope_s, scale_pre[:, :], "rope1_scaled", 1)

            def dilated(i, first):
                for g in range(4):
                    hd, c = 4 * i + g, C_QKV + 12 * i + 3 * g
                    s = (3 * g) % 4
                    lone = first and g == 0

                    def free():
                        dve.wait_ge(sem("scores_done"), at(hd))
                    sum_halves(c, s)
                    rotate_cos(c, s, rope_s)
                    if not lone:
                        ahead(c, s)
                    rotate(2 * hd, 2 * hd, rope_s, q_t, free)
                    sum_halves(c + 1, (s + 1) % 4)
                    rotate_cos(c + 1, (s + 1) % 4, rope_s)
                    ahead(c + 1, (s + 1) % 4)
                    rotate(2 * hd + 1, 2 * hd + 1, rope_s, k_t, free)
                    if not lone:
                        head_low_out(hd - 1)
                    sum_halves(c + 2, (s + 2) % 4)
                    dve.wait_ge(sem("v_turned"), at(hd))
                    scale_by(v_t[:, :], c + 2, s + 2, scale_pre[:, :], "v_scaled")
                    mask_max(hd, g % 2, mask_dil, float(P) ** -0.5)
                    ahead(c + 2, (s + 2) % 4)
                    normalise(hd, g % 2)

            def head_low_out(hd):
                dve.wait_ge(sem("inner_high"), 80 + hd + 1)
                V.tensor_copy(source[:, 0, :], head_out[:, 0:TOKENS]).then_inc(sem("out_read"), 1)
                dve.wait_ge(sem("out_read"), hd + 1)
                V.tensor_tensor(dyn2(inner, hd, 1), source[:, 0, :], dyn2(inner, hd, 0), ALU.subtract)\
                    .then_inc(sem("inner_ready"), 1)

            dilated(0, True)
            with dve.Fori(1, HEADS // 4) as i:
                dilated(i, False)
            head_low_out(HEADS - 1)
            out_section(C_OUT1)
            norm(2, 3, 5, C_MLP1)
            norm_scale(6, 3, 3)
            mlp_section(C_MLP1, 96, 64)

            with dve.Fori(0, LAYERS) as l:
                c0, u0, o0, v0, r0 = C_LAYER2 + N_LAYER2 * l, 16 + 28 * l, 16 + 16 * l, 16 + 9 * l, 8 + 8 * l
                rot0, gate0, split0, done0, sd0 = 32 + 22 * l, 16 * l, 160 + 16 * l, 16 + 24 * l, 4 + 5 * l
                cos0 = 32 + 18 * l

                norm(3 + l, 4 + l, r0 - 1, c0)
                norm_scale(r0, sd0, 4 + 7 * l)
                scaled_tables(rope2, rope_s, scale_pre[:, :], "rope2_scaled", l + 1)

                def gate_in(c, s, g):
                    if not isinstance(g, int) or g:
                        dve.wait_ge(sem("tanh_ready"), gate0 + g)
                    scale_by(scaled[:, 1, :], c, s, scale_pre[:, :], "gate_scaled")

                def gate_out(g, to=gate[:, :], used=0):
                    dve.wait_ge(sem("tanh_ready"), gate0 + g + 1)
                    dve.wait_ge(sem("source_ready"), 144 + gate0 + g - used)
                    V.scalar_tensor_tensor(out=to, in0=tanh_g[:, :], scalar=1.0, in1=scaled[:, 1, :],
                                           op0=ALU.add, op1=ALU.mult).then_inc(sem("gate_ready"), 1)

                def diff_finish(hd):
                    scale_out(r0 + 1 + hd, 5 + 7 * l + hd, scale_lat[:, 0, :])
                    V.scalar_tensor_tensor(out=normed[:, :], in0=head_out[:, 0:TOKENS], scalar=dyn_col(subln_gain, l),
                                           in1=scale_lat[:, 0, :], op0=ALU.mult, op1=ALU.mult)\
                        .then_inc(sem("out_read"), 1)
                    dve.wait_ge(sem("out_read"), o0 + hd + 1)
                    dve.wait_ge(sem("gate_ready"), gate0 + hd + 1)
                    V.scalar_tensor_tensor(out=source[:, 0, :], in0=normed[:, :], scalar=0.5, in1=gate[:, :],
                                           op0=ALU.mult, op1=ALU.mult).then_inc(sem("source_ready"), 1)

                def finish(o, g, done, gate_of=gate[:, :]):
                    dve.wait_ge(sem("head_done"), done)
                    V.tensor_copy(normed[:, :], head_out[:, 0:TOKENS]).then_inc(sem("out_read"), 1)
                    dve.wait_ge(sem("out_read"), o0 + o + 1)
                    dve.wait_ge(sem("gate_ready"), gate0 + g + 1)
                    V.scalar_tensor_tensor(out=source[:, 0, :], in0=normed[:, :], scalar=0.5, in1=gate_of,
                                           op0=ALU.mult, op1=ALU.mult).then_inc(sem("source_ready"), 1)

                def combine(hd):
                    u = u0 + 2 * hd
                    dve.wait_ge(sem("exp_ready"), 2 * u + 4)
                    V.reciprocal(small[:, 8:12], small[:, 4:8]).then_inc(sem("inverse_ready"), 2)
                    dve.wait_ge(sem("inverse_ready"), u + 2)
                    V.tensor_scalar(inverse(1), inverse(1), dyn_col(lam, l), None, ALU.mult).then_inc(sem("lam_inverse"), 1)
                    dve.wait_ge(sem("lam_inverse"), DA_HEADS * l + hd + 1)
                    for t, (lo, hi) in enumerate(((0, P), (P, COLS))):
                        op = V.tensor_scalar(prob[:, 1, lo:hi], prob[:, 1, lo:hi], inverse(1, t), None, ALU.mult)
                    op.then_inc(sem("second_scaled"), 1)
                    dve.wait_ge(sem("second_scaled"), DA_HEADS * l + hd + 1)
                    for t, (lo, hi) in enumerate(((0, P), (P, COLS))):
                        op = V.scalar_tensor_tensor(out=prob[:, 0, lo:hi], in0=prob[:, 0, lo:hi], scalar=inverse(0, t),
                                                    in1=prob[:, 1, lo:hi], op0=ALU.mult, op1=ALU.subtract)
                    op.then_inc(sem("prob_ready"), 2)

                def diff_mean(hd):
                    mean(r0 + 1 + hd, P, SUBLN_EPS, "stat_done", sd0 + hd + 2)

                def differential(hd, first):
                    c = c0 + 4 * hd

                    def free():
                        dve.wait_ge(sem("scores_done"), u0 + 2 * hd)
                    sum_halves(c, 0)
                    rotate_cos(c, 0, rope_s)
                    if not first:
                        ahead(c, 0)
                    rotate(rot0 + 2 * hd, cos0 + 2 * hd, rope_s, q_t, free)
                    sum_halves(c + 1, 1)
                    rotate_cos(c + 1, 1, rope_s)
                    ahead(c + 1, 1)
                    rotate(rot0 + 2 * hd + 1, cos0 + 2 * hd + 1, rope_s, k_t, free)
                    sum_halves(c + 2, 2)
                    dve.wait_ge(sem("v_turned"), v0 + hd)
                    scale_by(v_t[:, :], c + 2, 2, scale_pre[:, :], "v_scaled")
                    for j in range(2):
                        mask_max(u0 + 2 * hd + j, j, mask_causal, 64.0 ** -0.5)
                    ahead(c + 2, 2)
                    if not first:
                        diff_mean(hd - 1)
                    sum_halves(c + 3, 3)
                    gate_in(c + 3, 3, hd)
                    if not first:
                        diff_finish(hd - 1)
                    gate_out(hd)
                    combine(hd)
                    ahead(c + 3, 3)
                    if not first:
                        split_low(split0 + hd - 1, hd - 1, 0)

                differential(0, True)
                with dve.Fori(1, DA_HEADS) as hd:
                    differential(hd, False)

                c, hd = c0 + N_DA, DA_HEADS - 1

                def all_scored():
                    dve.wait_ge(sem("scores_done"), u0)
                sum_halves(c, 0)
                rotate_cos(c, 0, rope_s)
                ahead(c, 0, units=1)
                rotate(rot0 + 8, cos0 + 8, rope_s, kw_t, all_scored)
                sum_halves(c + 1, 1)
                dve.wait_ge(sem("v_turned"), v0 + DA_HEADS)
                scale_by(v_t[:, :], c + 1, 1, scale_pre[:, :], "v_scaled")
                ahead(c + 1, 1)
                sum_halves(c + 2, 2)
                rotate_cos(c + 2, 2, rope_s)
                ahead(c + 2, 2)
                rotate(rot0 + 9, cos0 + 9, rope_s, kr_t, all_scored)
                diff_mean(hd)
                sum_halves(c + 3, 3)
                dve.wait_ge(sem("v_ready"), v0 + DA_HEADS + 1)
                diff_finish(hd)
                ahead(c + 3, 3)
                split_low(split0 + hd, hd, 0)

                def window(i, first):
                    for g in range(2):
                        b, c = 2 * i + g, c0 + N_DA + N_KV + 4 * i + 2 * g
                        lone = first and g == 0

                        def free():
                            dve.wait_ge(sem("scores_done"), u0 + 8 + 2 * b)
                        sum_halves(c, 2 * g)
                        rotate_cos(c, 2 * g, rope_s)
                        ahead(c, 2 * g)
                        rotate(rot0 + 10 + b, cos0 + 10 + b, rope_s, q_t, free)
                        sum_halves(c + 1, 2 * g + 1)
                        gate_in(c + 1, 1, DA_HEADS + b)
                        if not lone:
                            finish(DA_HEADS + b - 1, DA_HEADS + b - 1, done0 + DA_HEADS + 2 * b)
                        gate_out(DA_HEADS + b)
                        for j in range(2):
                            mask_max(u0 + 8 + 2 * b + j, j, mask_window, 64.0 ** -0.5,
                                     neg_sink=(dyn_col(neg_sinks, 16 * l + 8 * j + b), 16 * l + 2 * b + j))
                        ahead(c + 1, 2 * g + 1)
                        for j in range(2):
                            normalise(u0 + 8 + 2 * b + j, j, sink=16 * l + 2 * b + j)
                        if not lone:
                            split_low(split0 + DA_HEADS + b - 1, DA_HEADS + b - 1, 0)

                window(0, True)
                with dve.Fori(1, SW_BLOCKS // 2) as i:
                    window(i, False)

                c = c0 + N_DA + N_KV + N_SW
                for i in range(N_LATENT):
                    sum_halves(c + i, i % 4)
                    if i > 1:
                        dve.wait_ge(sem("latent_squared"), N_LATENT * l + i - 1)
                    if i < 2:
                        dve.wait_ge(sem("tanh_ready"), gate0 + 12)
                    scale_by(scaled[:, i % 2, :], c + i, i, scale_pre[:, :], "latent_scaled")
                    if i == 1:
                        finish(11, 11, done0 + DA_HEADS + 2 * SW_BLOCKS)
                    ahead(c + i, i % 4)
                    dve.wait_ge(sem("latent_high"), N_LATENT * l + i + 1)
                    dve.wait_ge(sem("latent_scaled"), N_LATENT * l + i + 1)
                    V.scalar_tensor_tensor(out=latent[:, i, 1, :], in0=scaled[:, i % 2, :], scalar=latent_gain(l, i),
                                           in1=latent[:, i, 0, :], op0=ALU.mult, op1=ALU.subtract)\
                        .then_inc(sem("latent_ready"), 1)
                    if i == 1:
                        split_low(split0 + 11, 11, 0)
                    if i == LATENT:
                        mean(r0 + 5, LATENT * P, NORM_EPS, "latent_counted", N_LATENT * l + LATENT)
                    if i == LATENT + 1:
                        scale_out(r0 + 5, 9 + 7 * l, scale_lat[:, 0, :])
                        scaled_tables(rope2, rope_q, scale_lat[:, 0, :], "rope_q_scaled", l + 1)

                mla_gates = [gate[:, :], step[:, 0, :]]

                def mla_finish(hd):
                    finish(12 + hd, 12 + hd, done0 + 21 + hd, mla_gates[hd % 2])

                c = c + N_LATENT
                mean(r0 + 6, LATENT * P, NORM_EPS, "latent_counted", N_LATENT * (l + 1))
                for hd in range(MLA_HEADS):
                    s = (2 * hd) % 4
                    s3 = (s + 3) % 4
                    if hd > 1:
                        mla_finish(hd - 2)
                    if hd:
                        mask_max(u0 + 23 + hd, (hd - 1) % 2, mask_causal, 192.0 ** -0.5)
                    if hd > 1:
                        split_low(split0 + 10 + hd, 10 + hd, 0)
                    sum_halves(c + 2 * hd, s)
                    gate_in(c + 2 * hd, s, 12 + hd)
                    if hd:
                        normalise(u0 + 23 + hd, (hd - 1) % 2)
                    ahead(c + 2 * hd, s)
                    gate_out(12 + hd, mla_gates[hd % 2], int(hd > 0))
                    if hd == 0:
                        scale_out(r0 + 6, 10 + 7 * l, scale_lat[:, 1, :])
                    c_u = c + 2 * hd + 1
                    dve.wait_ge(corr_ready, c_u + 1)
                    dve.wait_ge(sem("swapped_ready"), rot0 + 19 + hd)
                    dve.wait_ge(sem("scores_done"), u0 + 24 + hd)
                    V.tensor_tensor(q_t[:, :], acc[s + 1][:, 0:TOKENS], scale_lat[:, 0, :], ALU.mult)
                    V.tensor_tensor(k_t[:, :], acc[s + 1][:, TOKENS:], scale_lat[:, 1, :], ALU.mult)\
                        .then_inc(sem("nope_ready"), 1)
                    V.tensor_tensor(turned[:, :], swapped[:, :], rope_q[:, 1, :], ALU.mult).then_inc(sem("rot_sin"), 1)
                    dve.wait_ge(sem("v_turned"), v0 + 5 + hd)
                    V.tensor_tensor(v_t[:, :], acc[s3][:, 0:TOKENS], scale_lat[:, 1, :], ALU.mult)\
                        .then_inc(sem("v_scaled"), 1)
                    V.tensor_tensor(scaled[:, 0, :], corr[:, 1, :], rope_q[:, 0, :], ALU.mult).then_inc(summed, 1)
                    dve.wait_ge(summed, c_u + 1)
                    dve.wait_ge(sem("rot_sin"), rot0 + 19 + hd)
                    V.tensor_tensor(qr_t[:, :], scaled[:, 0, :], turned[:, :], ALU.add).then_inc(sem("rotated"), 1)
                    ahead(c_u, s + 1)
                mla_finish(2)
                mask_max(u0 + 27, 1, mask_causal, 192.0 ** -0.5)
                split_low(split0 + 14, 14, 0)
                normalise(u0 + 27, 1)
                mla_finish(3)
                split_low(split0 + 15, 15, 0)
                out_section(c + N_MLA)
            norm(NORMS - 1, None, 23, None)


def weight_stream(w_in_ab, w_out_ab, w_qkv, w_o, w_up, w_down, w_in_2, w_uq_2, w_ukv_2, w_out_2):
    stream = np.zeros((LOADED, P, UNITS, P), np.float32)
    at = [0]

    def put(columns):
        stream[at[0]] = columns.reshape(UNITS, P, P).transpose(1, 0, 2)
        at[0] += 1

    def blocks(w, first, count=1, width=P):
        for i in range(count):
            put(w[:, first + width * i:first + width * (i + 1)])

    w = w_in_ab[0]
    width = A_BLOCKS * P
    blocks(w, width, A_BLOCKS)
    for j in range(A_BLOCKS):
        for part in (3, 4, 2, 0):
            blocks(w, part * width + P * j)
    blocks(w_out_ab[0], 0, KB)

    def mlp(layer):
        for q in range(FFN_QUARTERS):
            blocks(w_up[layer], D * q, KB)
            blocks(w_down[layer][D * q:D * (q + 1)], 0, KB)

    mlp(0)
    for hd in range(HEADS):
        for part in range(3):
            blocks(w_qkv[0], D * part + P * hd)
    blocks(w_o[0], 0, KB)
    mlp(1)

    half = P // 2
    for layer in range(LAYERS):
        w = w_in_2[layer]
        for hd in range(DA_HEADS):
            for first in (0, 512, 1024, 1536):
                blocks(w, first + P * hd)
        blocks(w, 3072)
        blocks(w, 3200)
        put(np.concatenate([w[:, 5376:5440]] * 2, 1))
        at[0] += 1
        for b in range(SW_BLOCKS):
            for first in (2048, 3328):
                put(np.concatenate([w[:, first + half * b:first + half * (b + 1)],
                                    w[:, first + half * (8 + b):first + half * (9 + b)]], 1))
        blocks(w, 4352, LATENT)
        blocks(w, 4864, LATENT)
        uq, ukv = w_uq_2[layer], w_ukv_2[layer]
        for hd in range(MLA_HEADS):
            blocks(w, 5440 + P * hd)
            pair = [192 * (2 * (hd // 2) + i) + P for i in range(2)]
            put(np.concatenate([uq[:, 192 * hd:192 * hd + P], ukv[:, 256 * hd:256 * hd + P],
                                ukv[:, 256 * hd + P:256 * (hd + 1)],
                                np.concatenate([uq[:, a:a + half] for a in pair], 1)]))
        order = list(range(512))
        for b in range(SW_BLOCKS):
            for first in (512 + half * b, 512 + half * (8 + b)):
                order += list(range(first, first + half))
        order += list(range(1536, D))
        blocks(w_out_2[layer][order], 0, KB)
    return stream.reshape(LOADED, P, UNITS * P)


def per_feature(sink_logits_2, gains_pre, gains_post, conv_w, q_norm, kv_norm, subln):
    col = np.zeros((P, N_COLS), np.float32)
    for i, g in enumerate(gains_pre):
        col[:, G_PRE + KB * i:G_PRE + KB * (i + 1)] = g.reshape(KB, P).T
    for i, g in enumerate(gains_post):
        col[:, G_POST + KB * i:G_POST + KB * (i + 1)] = g.reshape(KB, P).T
    col[:, CONV:CONV + 3 * A_BLOCKS] = conv_w[0].reshape(3 * A_BLOCKS, P).T
    col[:, Q_NORM:Q_NORM + LAYERS * LATENT] = q_norm.reshape(LAYERS * LATENT, P).T
    col[:, KV_NORM:KV_NORM + LAYERS * LATENT] = kv_norm.reshape(LAYERS * LATENT, P).T
    col[:, SUBLN:SUBLN + LAYERS] = subln.T
    col[:, SINK:SINK + 16 * LAYERS] = sink_logits_2.reshape(1, -1)
    p = np.arange(P)
    col[:, INV_FREQ] = (10000.0 ** (-(p % 32) * 2.0 / 64)).astype(np.float32)
    col[:, SIGN] = np.where(p % 64 < 32, -1, 1)
    for layer in range(LAYERS):
        lam_init = 0.8 - 0.6 * math.exp(-0.3 * layer)
        col[:, LAM_INIT + layer] = lam_init
        col[:, LAM_INIT + LAYERS + layer] = 1 - lam_init
    return col


def shape_tables():
    t, s = np.arange(TOKENS)[:, None], np.arange(TOKENS)[None, :]
    back = t - s
    count = sum(((back >= 0) & (back % dilation == 0) & (back // dilation <= window // dilation)).astype(int)
                for window, dilation in ((128, 1), (512, 4), (2048, 16)))
    masks = [np.where(count > 0, np.log(np.maximum(count, 1)), MASKED), np.where(back >= 0, 0, MASKED),
             np.where((back >= 0) & (back < 128), 0, MASKED)]
    parts = [np.eye(P), np.ones((P, P))]
    for m in masks:
        parts += [m[:P, :P], m[P:, :]]
    half = P // 2
    freq = np.float32(10000.0) ** (-np.arange(half, dtype=np.float32) * np.float32(2.0) / np.float32(P))
    angle = (np.arange(TOKENS, dtype=np.float32)[None, :] * freq.astype(np.float32)[:, None]).astype(np.float64)
    parts += [np.concatenate([np.cos(angle)] * 2), np.concatenate([-np.sin(angle), np.sin(angle)])]
    return np.ascontiguousarray(np.concatenate(parts, 1).astype(np.float32))


def kernel(x, norm_mix_pre, norm_mix_post, norm_mlp_pre, norm_mlp_post, w_in_ab, w_spatial, b_spatial,
           conv_w, w_out_ab, w_qkv, w_o, w_up, w_down, positions_2, pre_norm_w_2, post_norm_w_2,
           w_in_2, diff_lambda_q1_2, diff_lambda_k1_2, diff_lambda_q2_2, diff_lambda_k2_2,
           diff_subln_w_2, sink_logits_2, mla_q_norm_w_2, mla_kv_norm_w_2, w_uq_2, w_ukv_2, w_out_2):
    import concourse.bacc as _bacc
    from concourse.bass_utils import run_bass_kernel_spmd as _run

    gains_pre = [norm_mix_pre[0], norm_mlp_pre[0], norm_mix_pre[1], norm_mlp_pre[1], *pre_norm_w_2]
    gains_post = [norm_mix_post[0], norm_mlp_post[0], norm_mix_post[1], norm_mlp_post[1], *post_norm_w_2]
    lambdas = np.stack([diff_lambda_q1_2, diff_lambda_k1_2, diff_lambda_q2_2, diff_lambda_k2_2], 1)
    arrays = {
        "stream": weight_stream(w_in_ab, w_out_ab, w_qkv, w_o, w_up, w_down, w_in_2, w_uq_2, w_ukv_2, w_out_2),
        "x_t": np.ascontiguousarray(x[0].T.reshape(KB, P, TOKENS).transpose(1, 0, 2)),
        "columns": per_feature(sink_logits_2, gains_pre, gains_post, conv_w, mla_q_norm_w_2, mla_kv_norm_w_2,
                               diff_subln_w_2),
        "lambdas": np.ascontiguousarray(np.broadcast_to(lambdas.reshape(1, LAYERS, 256), (P, LAYERS, 256))),
        "w_spatial": np.ascontiguousarray(w_spatial[0].transpose(2, 0, 1)),
        "b_spatial": np.ascontiguousarray(np.broadcast_to(b_spatial, (P, A_BLOCKS, P))),
        "positions": np.ascontiguousarray(np.broadcast_to(positions_2, (P, TOKENS))),
        "tables": shape_tables(),
    }
    nc = _bacc.Bacc("TRN2", target_bir_lowering=False, num_devices=1)
    args = [nc.dram_tensor(name, a.shape, mybir.dt.from_np(a.dtype), kind="ExternalInput").ap()
            for name, a in arrays.items()]
    args.append(nc.dram_tensor("out_0", (P, KB, TOKENS), F32, kind="ExternalOutput").ap())
    build(nc, *args)
    r = _run(nc, [arrays], core_ids=[0])
    return r.results[0]["out_0"].transpose(2, 1, 0).reshape(1, TOKENS, D)
```
